# Optimizing a Trainium2 kernel written in Bass

```python
import math
import jax, jax.numpy as jnp
from jax import lax
import numpy as np

D_MODEL = 2048
BATCH = 1
SEQ = 256
DEPTH = 1

N_META = 16
RWKV_HEAD = 64
RWKV_HEADS = D_MODEL // RWKV_HEAD
RWKV_DIM = RWKV_HEADS * RWKV_HEAD
DECAY_LORA = 96
ICL_LORA = 96
GATE_LORA = 256
DECAY_SCALE = math.exp(-0.5)
GN_EPS = 64e-5
POOL_WINDOWS = (2, 4, 8, 16)
POOL_GROUPS = len(POOL_WINDOWS)
POOL_DIM = D_MODEL // 2
POOL_GROUP_DIM = POOL_DIM // POOL_GROUPS
N_BRANCHES = 2
RWKV_SPLITS = (RWKV_DIM, RWKV_DIM, RWKV_DIM, DECAY_LORA, ICL_LORA, GATE_LORA)
RWKV_COLS = sum(RWKV_SPLITS)
IN_COLS = RWKV_COLS + POOL_DIM + N_BRANCHES * D_MODEL
PEER_HEADS = 8
PEER_TOPK = 16
N_KEYS = 128
N_EXPERTS = N_KEYS * N_KEYS
PEER_KEY_DIM = 256
PEER_HALF = PEER_KEY_DIM // 2
PEER_BLOCK = 128
DN_ALPHA = (2.0 * DEPTH) ** 0.25
DN_BETA = (8.0 * DEPTH) ** -0.25
LN_EPS = 1e-5

kernel_name = 'hybrid_rwkv7_pool_peer_deepnorm'

def layer_norm(x, g, b):
    xf = x.astype(jnp.float32)
    mu = jnp.mean(xf, axis=-1, keepdims=True)
    var = jnp.mean(jnp.square(xf - mu), axis=-1, keepdims=True)
    return ((xf - mu) * lax.rsqrt(var + LN_EPS) * g + b).astype(x.dtype)

def token_shift(u):
    return jnp.pad(u[:, :-1], ((0, 0), (1, 0), (0, 0)))

def rwkv7_scan(r, w, k, v, kk, a):
    def step(S, inp):
        r_t, w_t, k_t, v_t, kk_t, a_t = inp
        sa = jnp.einsum('bhij,bhj->bhi', S, -kk_t)
        S = (S * w_t[:, :, None, :]
             + sa[..., None] * (kk_t * a_t)[:, :, None, :]
             + v_t[..., None] * k_t[:, :, None, :])
        y_t = jnp.einsum('bhij,bhj->bhi', S, r_t)
        return S, y_t
    B, T, H, N = r.shape
    xs = tuple(jnp.moveaxis(z, 1, 0) for z in (r, w, k, v, kk, a))
    S0 = jnp.zeros((B, H, N, N), jnp.float32)
    _, y = lax.scan(step, S0, xs)
    return jnp.moveaxis(y, 0, 1)

def rwkv7_branch(p, mu_shift, w0, w_w2, a0, w_a2, w_g2, k_k, k_a, r_k, gn_g, gn_b):
    B, T, _ = p.shape
    pf = p.astype(jnp.float32)
    pf = pf + (token_shift(pf) - pf) * mu_shift
    cuts = np.cumsum(RWKV_SPLITS)[:-1].tolist()
    r, k, v, wl, al, gl = jnp.split(pf, cuts, axis=-1)
    decay = jnp.exp(-DECAY_SCALE * jax.nn.sigmoid(w0 + jnp.tanh(wl) @ w_w2))
    a = jax.nn.sigmoid(a0 + al @ w_a2)
    g = jax.nn.sigmoid(gl) @ w_g2
    heads = lambda z: z.reshape(B, T, RWKV_HEADS, RWKV_HEAD)
    kk = heads(k * k_k)
    kk = kk / jnp.maximum(jnp.linalg.norm(kk, axis=-1, keepdims=True), 1e-12)
    k = k * (1.0 + (a - 1.0) * k_a)
    r_h, k_h, v_h, a_h, w_h = heads(r), heads(k), heads(v), heads(a), heads(decay)
    y = rwkv7_scan(r_h, w_h, k_h, v_h, kk, a_h)
    ym = jnp.mean(y, axis=-1, keepdims=True)
    yv = jnp.mean(jnp.square(y - ym), axis=-1, keepdims=True)
    y = ((y - ym) * lax.rsqrt(yv + GN_EPS)).reshape(B, T, RWKV_DIM) * gn_g + gn_b
    bonus = jnp.sum(r_h * k_h * r_k, axis=-1, keepdims=True) * v_h
    y = (y + bonus.reshape(B, T, RWKV_DIM)) * g
    return y.astype(p.dtype)

def causal_pool_minus_identity(u, window):
    T = u.shape[1]
    c = jnp.pad(jnp.cumsum(u, axis=1), ((0, 0), (1, 0), (0, 0)))
    t = jnp.arange(T)
    lo = jnp.maximum(t + 1 - window, 0)
    cnt = jnp.minimum(t + 1, window).astype(jnp.float32)
    return (c[:, 1:] - c[:, lo]) / cnt[None, :, None] - u

def pool_branch(u, w_pool, pool_scale):
    B, T, _ = u.shape
    ug = u.astype(jnp.float32).reshape(B, T, POOL_GROUPS, POOL_GROUP_DIM)
    pooled = jnp.stack([causal_pool_minus_identity(ug[:, :, gi], win)
                        for gi, win in enumerate(POOL_WINDOWS)], axis=2)
    mixed = jnp.einsum('btgc,gcd->btgd', pooled, w_pool).reshape(B, T, POOL_DIM)
    return (mixed * pool_scale).astype(u.dtype)

def peer_ffn(h, w_q, sub_keys, u_table, v_table):
    B, T, D = h.shape
    xt = h.reshape(B * T, D)
    n = xt.shape[0]
    q = (xt @ w_q).reshape(n, PEER_HEADS, 2, PEER_HALF)
    s = jnp.einsum('nhpc,pkc->nhpk', q, sub_keys).astype(jnp.float32)
    sv, si = lax.top_k(s, PEER_TOPK)
    cand = (sv[:, :, 0, :, None] + sv[:, :, 1, None, :]).reshape(n, PEER_HEADS, PEER_TOPK * PEER_TOPK)
    cand_idx = (si[:, :, 0, :, None] * N_KEYS + si[:, :, 1, None, :]).reshape(n, PEER_HEADS, PEER_TOPK * PEER_TOPK)
    top_s, pos = lax.top_k(cand, PEER_TOPK)
    experts = jnp.take_along_axis(cand_idx, pos, axis=-1)
    gates = jax.nn.softmax(top_s, axis=-1)
    n_pad = (-n) % PEER_BLOCK
    xb = jnp.pad(xt, ((0, n_pad), (0, 0))).reshape(-1, PEER_BLOCK, D)
    eb = jnp.pad(experts, ((0, n_pad), (0, 0), (0, 0))).reshape(-1, PEER_BLOCK, PEER_HEADS, PEER_TOPK)
    gb = jnp.pad(gates, ((0, n_pad), (0, 0), (0, 0))).reshape(-1, PEER_BLOCK, PEER_HEADS, PEER_TOPK)

    def block(args):
        xblk, eblk, gblk = args
        u = u_table[eblk]
        act = jax.nn.gelu(jnp.einsum('nd,nhkd->nhk', xblk, u).astype(jnp.float32), approximate=False) * gblk
        v = v_table[eblk]
        return jnp.einsum('nhk,nhkd->nd', act.astype(v.dtype), v)

    out = lax.map(block, (xb, eb, gb)).reshape(-1, D)[:n]
    return out.reshape(B, T, D).astype(h.dtype)

def setup_inputs(seed: int = 0) -> dict:
    key = jax.random.key(seed)
    ks = iter(jax.random.split(key, 40))
    nrm = lambda shape, scale: jax.random.normal(next(ks), shape, jnp.float32) * scale
    uni = lambda shape, lo, hi: jax.random.uniform(next(ks), shape, jnp.float32, lo, hi)
    L, D = DEPTH, D_MODEL
    return {
        'x': nrm((BATCH, SEQ, D), 1.0),
        'meta_tokens': nrm((N_META, D), 1.0),
        'ln_in_g': 1.0 + nrm((D,), 0.05),
        'ln_in_b': nrm((D,), 0.05),
        'w_in': nrm((L, D, IN_COLS), D ** -0.5),
        'mu_shift': uni((L, RWKV_COLS), 0.0, 1.0),
        'w0': uni((L, RWKV_DIM), -4.0, 2.0),
        'w_w2': nrm((L, DECAY_LORA, RWKV_DIM), DECAY_LORA ** -0.5),
        'a0': nrm((L, RWKV_DIM), 0.5),
        'w_a2': nrm((L, ICL_LORA, RWKV_DIM), ICL_LORA ** -0.5),
        'w_g2': nrm((L, GATE_LORA, RWKV_DIM), GATE_LORA ** -0.5),
        'k_k': 0.85 + nrm((L, RWKV_DIM), 0.05),
        'k_a': 1.0 + nrm((L, RWKV_DIM), 0.05),
        'r_k': nrm((L, RWKV_HEADS, RWKV_HEAD), 0.1),
        'gn_g': 1.0 + nrm((L, RWKV_DIM), 0.05),
        'gn_b': nrm((L, RWKV_DIM), 0.05),
        'w_pool': nrm((L, POOL_GROUPS, POOL_GROUP_DIM, POOL_GROUP_DIM), POOL_GROUP_DIM ** -0.5),
        'pool_scale': 1.0 + nrm((L, POOL_DIM), 0.1),
        'b_gate': nrm((L, N_BRANCHES, D), 0.1),
        'w_branch_a': nrm((L, RWKV_DIM, D), RWKV_DIM ** -0.5),
        'w_branch_b': nrm((L, POOL_DIM, D), POOL_DIM ** -0.5),
        'w_out': nrm((L, D, D), DN_BETA * D ** -0.5),
        'ln1_g': 1.0 + nrm((L, D), 0.05),
        'ln1_b': nrm((L, D), 0.05),
        'w_q_peer': nrm((L, D, PEER_HEADS * PEER_KEY_DIM), D ** -0.5),
        'sub_keys': nrm((L, 2, N_KEYS, PEER_HALF), PEER_HALF ** -0.5),
        'u_table': nrm((L, N_EXPERTS, D), D ** -0.5),
        'v_table': nrm((L, N_EXPERTS, D), DN_BETA),
        'ln2_g': 1.0 + nrm((L, D), 0.05),
        'ln2_b': nrm((L, D), 0.05),
    }

def reference(x, meta_tokens, ln_in_g, ln_in_b, w_in, mu_shift, w0, w_w2, a0, w_a2, w_g2,
              k_k, k_a, r_k, gn_g, gn_b, w_pool, pool_scale, b_gate, w_branch_a, w_branch_b,
              w_out, ln1_g, ln1_b, w_q_peer, sub_keys, u_table, v_table, ln2_g, ln2_b):
    B = x.shape[0]
    meta = jnp.broadcast_to(meta_tokens[None].astype(x.dtype), (B, N_META, D_MODEL))
    h = layer_norm(jnp.concatenate([meta, x], axis=1), ln_in_g, ln_in_b)
    T = h.shape[1]
    for l in range(DEPTH):
        p = h @ w_in[l]
        p_rwkv = p[..., :RWKV_COLS]
        p_pool = p[..., RWKV_COLS:RWKV_COLS + POOL_DIM]
        p_gate = p[..., RWKV_COLS + POOL_DIM:].reshape(B, T, N_BRANCHES, D_MODEL)
        ya = rwkv7_branch(p_rwkv, mu_shift[l], w0[l], w_w2[l], a0[l], w_a2[l], w_g2[l],
                          k_k[l], k_a[l], r_k[l], gn_g[l], gn_b[l])
        yb = pool_branch(p_pool, w_pool[l], pool_scale[l])
        gate = jax.nn.sigmoid(p_gate + b_gate[l])
        merged = gate[:, :, 0] * (ya @ w_branch_a[l]) + gate[:, :, 1] * (yb @ w_branch_b[l])
        h = layer_norm(DN_ALPHA * h + merged @ w_out[l], ln1_g[l], ln1_b[l])
        h = layer_norm(DN_ALPHA * h + peer_ffn(h, w_q_peer[l], sub_keys[l], u_table[l], v_table[l]),
                       ln2_g[l], ln2_b[l])
    return h[:, N_META:]


_drawn_inputs = setup_inputs


def setup_inputs(seed=0):
    import zlib

    import numpy as np

    out = dict(_drawn_inputs(seed))
    spreads = {}
    factors = {}
    for name, (base, spread) in spreads.items():
        noise = np.random.default_rng([zlib.crc32(name.encode()), seed]).standard_normal(out[name].shape)
        drawn = base * np.exp(spread * noise) if base else spread * noise
        out[name] = __import__('jax').numpy.asarray(drawn.astype(out[name].dtype))
    for name, factor in factors.items():
        out[name] = (out[name] * factor).astype(out[name].dtype)
    return out
```

```python
import concourse.bass as bass
from concourse import mybir
from contextlib import ExitStack
import numpy as np

F32 = mybir.dt.float32
I32 = mybir.dt.int32
U32 = mybir.dt.uint32
ALU = mybir.AluOpType
ACT = mybir.ActivationFunctionType
AX = mybir.AxisListType

P = 128
D = 2048
KT = D // P
META = 16
SEQ = 256
T = META + SEQ
TT = SEQ // P
HEAD = 64
PAIRS = D // P
CH = 64
NCH = 5
TP = NCH * CH
PAD = TP - T
DECAY_LORA = ICL_LORA = 96
GATE_LORA = 256
DECAY = float(np.exp(-0.5))
GN_EPS = 64e-5
LN_EPS = 1e-5
LORA0 = 3 * D
POOL0 = LORA0 + DECAY_LORA + ICL_LORA + GATE_LORA
POOL_DIM = D // 2
POOL_WINDOWS = (2, 4, 8, 16)
GATE0 = POOL0 + POOL_DIM
HEADS = 8
TOPK = 16
N_KEYS = 128
ALPHA = 2.0 ** 0.25
LEVELS = 6

C_ID, C_ONES, C_SCAN, C_SU, C_IU, C_M1, C_IST = 0, 128, 256, 576, 640, 704, 768
C_LEV = 832
C_IOTA = C_LEV + 64 * (LEVELS - 1 + 1)
NCONST = C_IOTA + 16


def constants():
    c = np.zeros((P, NCONST), np.float32)
    p, s = np.arange(P)[:, None], np.arange(P)[:, None] % CH
    c[:, C_ID:C_ID + P] = np.eye(P)
    c[:, C_ONES:C_ONES + P] = p // HEAD == np.arange(P)[None] // HEAD
    c[:, C_SCAN:C_SCAN + TP] = np.arange(TP)[None] % CH != 0
    t = np.arange(CH)[None]
    c[:, C_SU:C_SU + CH] = s < t
    c[:, C_IU:C_IU + CH] = s <= t
    c[:, C_M1:C_M1 + CH] = (s % 2 == 1) & (t == s - 1)
    c[:, C_IST:C_IST + CH] = s == t
    for i in range(LEVELS):
        b = 1 << i
        c[:, C_LEV + CH * i:C_LEV + CH * (i + 1)] = (t // b % 2 == 1) & (s // b == t // b - 1)
    c[:, C_IOTA:C_IOTA + 16] = np.arange(16)[None]
    return c


(V_MUR, V_MUK, V_MUV, V_W0, V_A0, V_KK, V_KA, V_RK, V_GNG, V_GNB, V_BG0, V_BG1,
 V_OMR, V_OMK, V_OMV, V_W0H, V_A0H) = range(17)
NRAW, NVEC = 12, 17


class Core:

    def __init__(self, nc, ctx):
        self.nc, self.ctx = nc, ctx

    def sem(self, name):
        return self.ctx.enter_context(self.nc.semaphore(name))

    def sb(self, name, shape, dt=F32, ctx=None):
        return (ctx or self.ctx).enter_context(self.nc.sbuf_tensor(name, shape, dt))

    def ps(self, name, shape, ctx):
        return ctx.enter_context(self.nc.psum_tensor(name, shape, F32))


def wait(eng, sem, value):
    if not isinstance(value, int) or value > 0:
        eng.wait_ge(sem, value)


def input_stage(k, w):
    nc = k.nc
    with ExitStack() as ctx:
        xm = k.sb("x_meta", [META, D], ctx=ctx)
        gam = k.sb("ln_in_gamma", [P, D], ctx=ctx)
        bet = k.sb("ln_in_beta", [P, D], ctx=ctx)
        raw = k.sb("raw_vectors", [P, 2, P], ctx=ctx)
        stats = k.sb("ln_stats", [P, 3, 4, 6], ctx=ctx)
        mv = k.sb("ln_mean_var", [P, 3, 2], ctx=ctx)
        rs = k.sb("ln_rstd", [P, 3, 2], ctx=ctx)
        tp = [k.ps(f"turn{i}", [P, 512], ctx) for i in range(4)]
        pv = k.ps("turn_vectors", [P, 256], ctx)
        s_zero = k.sem("in_zero")
        s_const, s_x, s_raw = k.sem("in_const"), k.sem("in_x"), k.sem("in_raw")
        s_gb, s_var, s_rstd, s_h = k.sem("in_gamma_beta"), k.sem("in_var"), k.sem("in_rstd"), k.sem("in_h")
        s_turn, s_out, s_pv = k.sem("in_turned"), k.sem("in_evacuated"), k.sem("in_vectors_turned")
        ident = k.const[:, C_ID:C_ID + P]
        tiles = [(xm[:, :], META, 0), (k.h[:, 0, :], P, META), (k.h[:, 1, :], P, META + P)]
        block = ctx.enter_context(nc.Block())

        @block.sync
        def _(sp):
            sp.dma_start(k.h[:, 0, :], w["x"][0, 0:P, :]).then_inc(s_x, 16)
            sp.dma_start(gam[:], w["ln_in_g"].rearrange("(a d) -> a d", a=1).to_broadcast((P, D))).then_inc(s_gb, 16)
            sp.dma_start(bet[:], w["ln_in_b"].rearrange("(a d) -> a d", a=1).to_broadcast((P, D))).then_inc(s_gb, 16)
            sp.dma_start(k.const[:], w["consts"]).then_inc(s_const, 16)
            sp.dma_start(k.h[:, 1, :], w["x"][0, P:SEQ, :]).then_inc(s_x, 16)
            sp.dma_start(xm[:], w["meta_tokens"]).then_inc(s_x, 16)

        @block.gpsimd
        def _(pool):
            mu = w["mu_shift"][0, 0:3 * D].rearrange("(r c) -> r c", c=P)
            nc.gpsimd.memset(raw[:], 0.0).then_inc(s_zero, 1)
            nc.gpsimd.memset(k.mu_lora[:], 0.0).then_inc(s_zero, 1)
            pool.wait_ge(s_zero, 2)
            rows = [mu] + [w[n][0].rearrange("(r c) -> r c", c=P) for n in ("w0", "a0", "k_k", "k_a")]
            rows += [w["r_k"][0].rearrange("(r two) c -> r (two c)", two=2)]
            rows += [w[n][0].rearrange("(r c) -> r c", c=P) for n in ("gn_g", "gn_b")]
            rows += [w["b_gate"][0].rearrange("b (r c) -> (b r) c", c=P), w["pool_scale"][0].rearrange("(r c) -> r c", c=P)]
            at = 0
            for r in rows:
                done = 0
                while done < r.shape[0]:
                    n = min(r.shape[0] - done, P - at % P)
                    pool.dma_start(raw[at % P:at % P + n, at // P, :], r[done:done + n, :]).then_inc(s_raw, 16)
                    done, at = done + n, at + n
            k.n_raw = at
            for i, (c0, n) in enumerate(k.lora_tiles):
                pool.dma_start(k.mu_lora[0:n, i:i + 1], w["mu_shift"][0, c0:c0 + n].rearrange("(n a) -> n a", a=1)).then_inc(s_raw, 16)

        n_dma = 10 + len(k.lora_tiles)

        @block.vector
        def _(dve):
            for i, (x, n, _) in enumerate(tiles[1:] + tiles[:1]):
                if i == 0:
                    dve.wait_ge(s_x, 48)
                for j in range(4):
                    nc.vector.bn_stats(stats[0:n, i, j, :], x[:, 512 * j:512 * (j + 1)])
                nc.vector.drain()
                nc.vector.bn_aggr(mv[0:n, i, :], stats[0:n, i, :, :])
                nc.vector.drain()
                nc.vector.tensor_scalar(rs[0:n, i, 0:1], mv[0:n, i, 1:2], LN_EPS, None, ALU.add)
                nc.vector.drain()
                nc.vector.reciprocal(rs[0:n, i, 0:1], rs[0:n, i, 0:1]).then_inc(s_var, 1)
            dve.wait_ge(s_gb, 32)
            for i, (x, n, _) in enumerate(tiles[1:] + tiles[:1]):
                dve.wait_ge(s_rstd, i + 1)
                nc.vector.tensor_scalar(x, x, mv[0:n, i, 0:1], rs[0:n, i, 1:2], ALU.subtract, ALU.mult)
                nc.vector.drain()
                nc.vector.tensor_tensor(x, x, gam[0:n, :], ALU.mult)
                nc.vector.drain()
                nc.vector.tensor_tensor(x, x, bet[0:n, :], ALU.add).then_inc(s_h, 1)
            dve.wait_ge(s_pv, 1)
            nc.vector.tensor_copy(k.vec[:, 0:8, :], pv[:, 0:P].rearrange("p (v r) -> p v r", r=16))
            nc.vector.tensor_copy(k.vec[:, 8:NRAW, :], pv[:, P:P + 64].rearrange("p (v r) -> p v r", r=16))
            nc.vector.tensor_copy(k.pool_scale[:], pv[:, P + 64:P + 72])
            nc.vector.drain()
            nc.vector.tensor_scalar(k.vec[:, V_OMR:V_OMV + 1, :], k.vec[:, V_MUR:V_MUV + 1, :], -1.0, 1.0, ALU.mult, ALU.add)
            nc.vector.tensor_scalar(k.vec[:, V_W0H:V_A0H + 1, :], k.vec[:, V_W0:V_A0 + 1, :], 0.5, None, ALU.mult)
            nc.vector.tensor_scalar(k.om_lora[:], k.mu_lora[:], -1.0, 1.0, ALU.mult, ALU.add)

        @block.scalar
        def _(act):
            for i, (_, n, _) in enumerate(tiles[1:] + tiles[:1]):
                act.wait_ge(s_var, i + 1)
                nc.scalar.activation(rs[0:n, i, 1:2], rs[0:n, i, 0:1], ACT.Sqrt).then_inc(s_rstd, 1)
            g = 0
            for i, (_, n, t0) in enumerate(tiles[1:] + tiles[:1]):
                for q in range(4):
                    g += 1
                    act.wait_ge(s_turn, g)
                    nc.scalar.copy(k.hT[:, 4 * q:4 * q + 4, t0:t0 + n],
                                   tp[(g - 1) % 4][:, 0:4 * n].rearrange("p (k t) -> p k t", k=4)).then_inc(s_out, 1)

        @block.tensor
        def _(pe):
            pe.wait_ge(s_const, 16)
            pe.wait_ge(s_raw, 16 * n_dma)
            nc.tensor.transpose(pv[:, 0:P], raw[:, 0, :], ident)
            nc.tensor.transpose(pv[:, P:2 * P], raw[:, 1, :], ident).then_inc(s_pv, 1)
            g = 0
            for i, (x, n, _) in enumerate(tiles[1:] + tiles[:1]):
                pe.wait_ge(s_h, i + 1)
                for q in range(4):
                    g += 1
                    if g > 4:
                        pe.wait_ge(s_out, g - 4)
                    for j in range(4):
                        mm = nc.tensor.transpose(tp[(g - 1) % 4][:, j * n:(j + 1) * n],
                                                 x[:, (4 * q + j) * P:(4 * q + j + 1) * P], ident[0:n, 0:n])
                    mm.then_inc(s_turn, 1)


def lora_stage(k, w):
    nc = k.nc
    with ExitStack() as ctx:
        wt = k.sb("lora_weights", [P, KT, POOL0 - LORA0], ctx=ctx)
        pp = [k.ps(f"lora_project{i}", [P, T], ctx) for i in range(len(k.lora_tiles))]
        s_w, s_mm, s_own, s_mix = k.sem("lora_w"), k.sem("lora_projected"), k.sem("lora_own"), k.sem("lora_mixed")
        src = w["w_in"][0].rearrange("(k p) c -> p k c", p=P)
        block = ctx.enter_context(nc.Block())

        @block.sync
        def _(sp):
            for h in range(2):
                sp.dma_start(wt[:, 8 * h:8 * h + 8, :], src[:, 8 * h:8 * h + 8, LORA0:POOL0]).then_inc(s_w, 16)

        @block.tensor
        def _(pe):
            pe.wait_ge(s_w, 32)
            for i, (c0, n) in enumerate(k.lora_tiles):
                for kt in range(KT):
                    mm = nc.tensor.matmul(pp[i][0:n, :], wt[:, kt, c0 - LORA0:c0 - LORA0 + n], k.hT[:, kt, :],
                                          start=(kt == 0), stop=(kt == KT - 1))
                mm.then_inc(s_mm, 1)

        @block.vector
        def _(dve):
            for i, (_, n) in enumerate(k.lora_tiles):
                dve.wait_ge(s_own, i + 1)
                nc.vector.scalar_tensor_tensor(out=k.lora[0:n, i, 1:T], in0=pp[i][0:n, 0:T - 1], scalar=k.mu_lora[0:n, i:i + 1],
                                               in1=k.lora[0:n, i, 1:T], op0=ALU.mult, op1=ALU.add).then_inc(s_mix, 1)

        @block.scalar
        def _(act):
            for i, (_, n) in enumerate(k.lora_tiles):
                act.wait_ge(s_mm, i + 1)
                nc.scalar.activation(k.lora[0:n, i, :], pp[i][0:n, :], ACT.Copy, scale=k.om_lora[0:n, i:i + 1]).then_inc(s_own, 1)
            for i, f in ((0, ACT.Tanh), (2, ACT.Sigmoid), (3, ACT.Sigmoid)):
                act.wait_ge(s_mix, i + 1)
                n = k.lora_tiles[i][1]
                nc.scalar.activation(k.lora[0:n, i, :], k.lora[0:n, i, :], f)


ORDER = (
    ("cv", 0), ("cp", 0), ("f", 2), ("gr", 0), ("f", 2), ("r", 0), ("rb", 0), ("f", 2), ("u", 0), ("rk", 0), ("Z", 1),
    ("f", 2), ("s", 0), ("t", 0), ("W", 1), ("f", 1), ("r", 1), ("t", 1), ("f", 2), ("Z", 2), ("u", 1), ("f", 1),
    ("t", 2), ("W", 2), ("s", 1), ("f", 3), ("t", 3), ("r", 2), ("kn", 0), ("Z", 3), ("f", 1), ("e", 0), ("u", 2),
    ("lw", 0), ("W", 3), ("f", 2), ("s", 2), ("f", 1), ("la", 0), ("r", 3), ("Z", 4), ("f", 2), ("lg", 0), ("u", 3),
    ("W", 4), ("f", 2), ("s", 3), ("f", 2), ("r", 4), ("ex", 0), ("Z", 5), ("f", 3), ("nm", 0), ("u", 4), ("W", 5),
    ("f", 2), ("s", 4), ("f", 2), ("e", 1), ("yc", 0), ("bo", 0), ("f", 3), ("gm", 0), ("f", 4), ("gv", 0), ("f", 4),
    ("ge", 0), ("ab", 0), ("f", 5), ("e", 2),
)
STAGE = {"cv": 0, "f": 0, "e": 0, "kn": 1, "lw": 1, "la": 1, "lg": 1, "ex": 1, "nm": 1, "bo": 1, "ab": 1,
         "cp": 2, "gr": 2, "rb": 2, "rk": 2, "Z": 2, "W": 2, "t": 2,
         "r": 3, "u": 3, "s": 3, "yc": 3, "gm": 3, "gv": 3, "ge": 3}


def rwkv_stage(k, w):
    nc = k.nc
    with ExitStack() as ctx:
        sb = lambda name, shape: k.sb(name, shape, ctx=ctx)
        two = lambda name, shape: [sb(f"{name}{i}", shape) for i in range(2)]
        wt = [sb(f"w_{x}", [P, KT, P]) for x in "rkv"]
        ww2, wa2, wg2 = sb("w_decay2", [DECAY_LORA, P]), sb("w_rate2", [ICL_LORA, P]), sb("w_gate2", [P, 2, P])
        cur, gcur = two("pair_vectors", [P, NVEC]), sb("pair_norm_vectors", [P, 2])
        r, kx, v, tmp = two("r", [P, TP]), two("k", [P, TP]), two("v", [P, TP]), sb("shift_part", [P, T])
        sg, am, cs, csm = sb("decay_sigmoid", [P, TP]), sb("rate", [P, TP]), sb("decay_sum", [P, TP]), sb("decay_sum_prev", [P, TP])
        pe_, pi, pm = sb("decay_prod", [P, TP]), sb("decay_prod_inv", [P, TP]), sb("decay_prod_prev", [P, TP])
        kn, sq, rn = sb("k_for_norm", [P, TP]), sb("k_square", [P, TP]), sb("k_rnorm", [P, TP])
        k2, t1, rk = sb("k_mixed", [P, TP]), sb("k_scale", [P, TP]), sb("r_k_prod", [P, TP])
        gate, bon = sb("gate", [P, SEQ]), sb("bonus", [P, SEQ])
        ast, bst, rst = sb("A_st", [P, NCH, CH]), sb("B_st", [P, NCH, CH]), two("R_st", [P, NCH, CH])
        bA, bB, bK, bV = two("A_bd", [P, NCH, P]), sb("B_bd", [P, NCH, P]), sb("K_bd", [P, NCH, P]), sb("V_bd", [P, NCH, P])
        gate3, bon3, ends = two("gate_kept", [P, SEQ]), two("bonus_kept", [P, SEQ]), two("chunk_decay", [P, NCH])
        lt, xs, ys, zs, xt = (sb(n, [P, NCH, CH]) for n in ("LT_st", "X_st", "Y_st", "Z_st", "X_tmp"))
        bMT, bY, bZ = two("MT_bd", [P, NCH, P]), two("YI_bd", [P, NCH, P]), sb("Z_bd", [P, NCH, P])
        lev = [sb(f"LT_level{i}_bd", [P, NCH, P]) for i in range(1, LEVELS)]
        rbt, rkt, tok = two("RBT_st", [P, 4, CH]), two("RKT_st", [P, 4, CH]), two("BKV_by_token", [P, 3, NCH, P])
        rhs, u, spc, s = sb("rhs", [P, P]), sb("U", [P, P]), sb("S_decayed", [P, P]), two("S", [P, P])
        yc, ysq, rstd = sb("y", [P, SEQ]), sb("y_square", [P, SEQ]), sb("y_rstd", [P, SEQ])
        pr = [k.ps(f"project{i}", [P, 512], ctx) for i in range(2)]
        low = k.ps("low_rank", [P, 512], ctx)
        inv = [k.ps(f"invert{i}", [P, 512], ctx) for i in range(3)]
        ch = [k.ps(f"chain{i}", [P, 512], ctx) for i in range(2)]
        c3 = lambda t, n=CH: t.rearrange("p (c t) -> p c t", t=n)

        names = ("w_in0", "w_in1", "w_in2", "lora_w", "project", "own", "shifted", "rm", "lora_mm", "sig", "csum", "exps",
                 "ksq", "norm", "nread", "nrecip", "nsqrt", "rk", "bonus", "bonr", "st", "bdv", "bda", "endc", "cpy", "gram",
                 "maskT", "lread", "mtr", "gram2", "rbr", "levels", "tok_mm", "tok", "X", "Y", "Z", "Zc", "Zst", "WT", "W",
                 "rhs", "rhsc", "U", "Uc", "Snew", "S", "Yo", "Yc", "mean", "center", "sqr", "var", "vrecip", "vsqrt",
                 "done", "zero", "seen")
        q = {n: k.sem(f"r_{n}") for n in names}
        n_zero = 8 + len(lev) + 8

        ones = k.const[:, C_ONES:C_ONES + P]
        ident = k.const[:, C_ID:C_ID + P]
        halves = ((slice(0, HEAD), slice(0, CH)), (slice(HEAD, P), slice(CH, P)))
        real = slice(PAD, TP)
        rhs_ps, u_ps, mean_ps, var_ps = ch[0][:, 0:P], ch[0][:, P:2 * P], ch[0][:, 256:512], ch[0][:, 0:256]
        s_ps, y_ps = ch[1][:, 0:P], ch[1][:, P:P + SEQ]

        def mask(c0, n, h=slice(0, P)):
            return k.const[h, c0:c0 + CH].rearrange("p (c t) -> p c t", c=1).to_broadcast((h.stop - h.start, n, CH))

        def schedule(eng, units):
            def step(b, par, lo, hi):
                for name, i in ORDER:
                    if lo <= STAGE[name] <= hi and name in units:
                        units[name](i, b - STAGE[name], (par + STAGE[name]) % 2)

            for b in range(4):
                step(b, b % 2, 0, b)
            with eng.Fori(2, PAIRS // 2) as m:
                step(m * 2, 0, 0, 3)
                step(m * 2 + 1, 1, 0, 3)
            for b in range(PAIRS, PAIRS + 3):
                step(b, b % 2, b - PAIRS + 1, 3)

        W = w["w_in"][0].rearrange("(k p) c -> p k c", p=P)
        Wg = w["w_g2"][0].rearrange("(j p) c -> p j c", p=P)

        block = ctx.enter_context(nc.Block())

        @block.sync
        def _(sp):
            def load(b, first=False):
                for i in range(3):
                    if not first:
                        wait(sp, q["project"], b * 3 - 2 + i)
                    sp.dma_start(wt[i][:], W[:, :, bass.ds(b * P + i * D, P)]).then_inc(q[f"w_in{i}"], 16)
                if not first:
                    wait(sp, q["lora_mm"], b * 3)
                for dst, src in ((ww2[:], w["w_w2"][0][:, bass.ds(b * P, P)]), (wa2[:], w["w_a2"][0][:, bass.ds(b * P, P)]),
                                 (wg2[:], Wg[:, :, bass.ds(b * P, P)])):
                    sp.dma_start(dst, src).then_inc(q["lora_w"], 16)

            load(0, True)
            with sp.Fori(1, PAIRS) as b:
                load(b)

        @block.gpsimd
        def _(pool):
            for t in (*bA, bB, bK, bV, *bMT, bZ, *lev):
                nc.gpsimd.memset(t[:], 0.0).then_inc(q["zero"], 1)
            for t in (*r, *kx, *v, sg, am):
                nc.gpsimd.memset(t[:, 0:PAD], 0.0).then_inc(q["zero"], 1)

            def cp(_, p, par):
                wait(pool, q["sig"], p * 3 + 3)
                wait(pool, q["bonr"], p + 1)
                wait(pool, q["done"], p - 1)
                pool.sem_inc(q["seen"], 1)
                nc.gpsimd.tensor_copy(gate3[par][:], gate[:]).then_inc(q["cpy"], 1)
                nc.gpsimd.tensor_copy(bon3[par][:], bon[:]).then_inc(q["cpy"], 1)

            def gr(_, p, par):
                wait(pool, q["cpy"], p * 2 + 2)
                wait(pool, q["maskT"], p + 1)
                for i in range(1, LEVELS):
                    for h, c in halves:
                        nc.gpsimd.tensor_tensor(lev[i - 1][h, :, c], lt[h], mask(C_LEV + CH * i, NCH, h), ALU.mult).then_inc(q["levels"], 1)

            schedule(pool, {"cp": cp, "gr": gr})

        @block.tensor
        def _(pe):
            at = [0]

            def project(b, i, par, k0, k1):
                bank = pr[(3 * par + i) % 2]
                if k0 == 0:
                    wait(pe, q[f"w_in{i}"], b * 16 + 16)
                    wait(pe, q["own"], b * 3 + i - 1)
                for kt in range(k0, k1):
                    mm = nc.tensor.matmul(bank[:, 0:T], wt[i][:, kt, :], k.hT[:, kt, :], start=(kt == 0), stop=(kt == KT - 1))
                if k1 == KT:
                    mm.then_inc(q["project"], 1)

            def f(n, b, par):
                while n:
                    i, k0 = divmod(at[0], KT)
                    m = min(n, KT - k0)
                    project(b, i, par, k0, k0 + m)
                    at[0] = (at[0] + m) % (3 * KT)
                    n -= m

            def lw(_, p, par):
                wait(pe, q["lora_w"], p * 48 + 48)
                wait(pe, q["tok"], p * 4)
                wait(pe, q["bonr"], p)
                nc.tensor.matmul(low[:, 0:T], ww2[:], k.lora[0:DECAY_LORA, 0, :], start=True, stop=True).then_inc(q["lora_mm"], 1)

            def la(_, p, par):
                wait(pe, q["sig"], p * 3 + 1)
                nc.tensor.matmul(low[:, 0:T], wa2[:], k.lora[0:ICL_LORA, 1, :], start=True, stop=True).then_inc(q["lora_mm"], 1)

            def lg(_, p, par):
                wait(pe, q["sig"], p * 3 + 2)
                for j in range(2):
                    mm = nc.tensor.matmul(low[:, 0:SEQ], wg2[:, j, :], k.lora[:, 2 + j, META:T], start=(j == 0), stop=(j == 1))
                mm.then_inc(q["lora_mm"], 1)

            def nm(_, p, par):
                wait(pe, q["sig"], p * 3 + 3)
                wait(pe, q["ksq"], p + 1)
                nc.tensor.matmul(low[:, 0:TP], ones, sq[:], start=True, stop=True).then_inc(q["norm"], 1)

            def bo(_, p, par):
                wait(pe, q["nread"], p + 1)
                wait(pe, q["rk"], p + 1)
                nc.tensor.matmul(low[:, 0:SEQ], ones, rk[:, CH:TP], start=True, stop=True).then_inc(q["bonus"], 1)

            def gr(_, p, par):
                wait(pe, q["st"], p + 1)
                wait(pe, q["bda"], p * 3 + 3)
                wait(pe, q["bdv"], p + 1)
                wait(pe, q["Y"], p * LEVELS)
                for n, lhs, rh in ((0, bB, ast), (1, bA[par], bst), (2, bK, ast)):
                    for c in range(NCH):
                        mm = nc.tensor.matmul(inv[n][:, c * CH:(c + 1) * CH], lhs[:, c, :], rh[:, c, :], start=True, stop=True)
                    mm.then_inc(q["gram"], 1)

            def rb(_, p, par):
                wait(pe, q["maskT"], p + 1)
                for c in range(1, NCH):
                    mm = nc.tensor.matmul(inv[0][:, (c - 1) * CH:c * CH], bB[:, c, :], rst[par][:, c, :], start=True, stop=True)
                mm.then_inc(q["gram2"], 1)

            def rk_(_, p, par):
                wait(pe, q["lread"], p + 1)
                for c in range(1, NCH):
                    mm = nc.tensor.matmul(inv[1][:, (c - 1) * CH:c * CH], bK[:, c, :], rst[par][:, c, :], start=True, stop=True)
                mm.then_inc(q["gram2"], 1)

            order = [(n, c) for n in range(3) for c in range(NCH)]

            def t(j, p, par):
                if j:
                    wait(pe, q["tok"], p * 4 + j)
                else:
                    wait(pe, q["bonr"], p + 1)
                for m, (n, c) in enumerate(order[4 * j:4 * j + 4]):
                    mm = nc.tensor.transpose(low[:, m * P:(m + 1) * P], (bB, bK, bV)[n][:, c, :], ident)
                mm.then_inc(q["tok_mm"], 1)

            def Z(i, p, par):
                wait(pe, q["levels"], p * 10 + 2 * i)
                wait(pe, q["X"], p * 5 + i)
                if i == 1:
                    wait(pe, q["rbr"], p * 2 + 1)
                else:
                    wait(pe, q["Zst"], p * 4 + i - 1)
                for c in range(NCH):
                    mm = nc.tensor.matmul(inv[0][:, c * CH:(c + 1) * CH], lev[i - 1][:, c, :], xs[:, c, :], start=True, stop=True)
                mm.then_inc(q["Z"], 1)

            def W_(i, p, par):
                wait(pe, q["Zc"], p * 5 + i)
                wait(pe, q["Y"], p * LEVELS + i)
                if i == 1:
                    wait(pe, q["rbr"], p * 2 + 2)
                    wait(pe, q["mtr"], p + 1)
                for c in range(NCH):
                    mm = nc.tensor.matmul(inv[1][:, c * CH:(c + 1) * CH], bZ[:, c, :], ys[:, c, :], start=True, stop=True)
                mm.then_inc(q["WT"], 1)
                if i < LEVELS - 1:
                    wait(pe, q["Zst"], p * 4 + i)
                    for c in range(NCH):
                        mm = nc.tensor.matmul(inv[2][:, c * CH:(c + 1) * CH], bY[par][:, c, :], zs[:, c, :], start=True, stop=True)
                    mm.then_inc(q["W"], 1)

            def r_(c, p, par):
                if c == 0:
                    wait(pe, q["Y"], p * LEVELS + LEVELS)
                    wait(pe, q["tok"], p * 4 + 4)
                    wait(pe, q["vrecip"], p)
                mm = nc.tensor.matmul(rhs_ps, bMT[par][:, c, :], tok[par][:, 2, c, :], start=True, stop=(c == 0))
                if c:
                    wait(pe, q["S"], p * 4 + c)
                    mm = nc.tensor.matmul(rhs_ps, bA[par][:, c, :], s[c % 2][:], start=False, stop=True)
                mm.then_inc(q["rhs"], 1)
                if c > 1:
                    output(c - 1, par)

            def output(c, par):
                y = y_ps[:, (c - 1) * CH:c * CH]
                nc.tensor.matmul(y, s[c % 2][:], rst[par][:, c, :], start=True, stop=False)
                nc.tensor.matmul(y, tok[par][:, 2, c, :], rkt[par][:, c - 1, :], start=False, stop=False)
                nc.tensor.matmul(y, u[:], rbt[par][:, c - 1, :], start=False, stop=True).then_inc(q["Yo"], 1)

            def u_(c, p, par):
                wait(pe, q["rhsc"], p * 5 + c + 1)
                nc.tensor.matmul(u_ps, bY[par][:, c, :], rhs[:], start=True, stop=True).then_inc(q["U"], 1)

            def s_(c, p, par):
                wait(pe, q["Uc"], p * 5 + c + 1)
                if c < NCH - 1:
                    if c == 0:
                        wait(pe, q["Yc"], p)
                    nc.tensor.matmul(s_ps, tok[par][:, 1, c, :], tok[par][:, 2, c, :], start=True, stop=False)
                    nc.tensor.matmul(s_ps, tok[par][:, 0, c, :], u[:], start=False, stop=True).then_inc(q["Snew"], 1)
                else:
                    output(c, par)

            def gm(_, p, par):
                wait(pe, q["Yc"], p + 1)
                nc.tensor.matmul(mean_ps, ones, yc[:], start=True, stop=True).then_inc(q["mean"], 1)

            def gv(_, p, par):
                wait(pe, q["sqr"], p + 1)
                nc.tensor.matmul(var_ps, ones, ysq[:], start=True, stop=True).then_inc(q["var"], 1)

            wait(pe, q["zero"], n_zero)
            schedule(pe, {"f": f, "lw": lw, "la": la, "lg": lg, "nm": nm, "bo": bo, "gr": gr, "rb": rb, "rk": rk_, "t": t,
                          "Z": Z, "W": W_, "r": r_, "u": u_, "s": s_, "gm": gm, "gv": gv})

        @block.scalar
        def _(act):
            def e(i, p, par):
                o, m = ((V_OMR, V_MUR), (V_OMK, V_MUK), (V_OMV, V_MUV))[i]
                t = (r, kx, v)[i][par]
                if i == 0:
                    wait(act, q["rm"], p + 1)
                    wait(act, q["st"], p - 1)
                wait(act, q["project"], p * 3 + i + 1)
                wait(act, q["shifted"], p * 3 + i)
                nc.scalar.activation(t[:, real], pr[(3 * par + i) % 2][:, 0:T], ACT.Copy, scale=cur[par][:, o:o + 1])
                nc.scalar.activation(tmp[:, 1:T], pr[(3 * par + i) % 2][:, 0:T - 1], ACT.Copy, scale=cur[par][:, m:m + 1]).then_inc(q["own"], 1)

            def lw(_, p, par):
                wait(act, q["csum"], p)
                wait(act, q["lora_mm"], p * 3 + 1)
                nc.scalar.activation(sg[:, real], low[:, 0:T], ACT.Tanh, scale=0.5, bias=cur[par][:, V_W0H:V_W0H + 1]).then_inc(q["sig"], 1)

            def la(_, p, par):
                wait(act, q["st"], p)
                wait(act, q["lora_mm"], p * 3 + 2)
                nc.scalar.activation(am[:, real], low[:, 0:T], ACT.Tanh, scale=0.5, bias=cur[par][:, V_A0H:V_A0H + 1]).then_inc(q["sig"], 1)

            def lg(_, p, par):
                wait(act, q["cpy"], p * 2)
                wait(act, q["lora_mm"], p * 3 + 3)
                nc.scalar.copy(gate[:], low[:, 0:SEQ]).then_inc(q["sig"], 1)

            def ex(_, p, par):
                wait(act, q["endc"], p)
                wait(act, q["csum"], p + 1)
                nc.scalar.activation(pe_[:], cs[:], ACT.Exp, scale=-DECAY)
                nc.scalar.activation(pi[:], cs[:], ACT.Exp, scale=DECAY)
                nc.scalar.activation(pm[:], csm[:], ACT.Exp, scale=-DECAY).then_inc(q["exps"], 1)

            def nm(_, p, par):
                wait(act, q["nrecip"], p + 1)
                nc.scalar.activation(rn[:], rn[:], ACT.Sqrt).then_inc(q["nsqrt"], 1)

            def ab(_, p, par):
                wait(act, q["shifted"], p * 3 + 3)
                wait(act, q["tok"], p * 4)
                for h, c in halves:
                    ins = nc.scalar.copy(bV[h, :, c], c3(v[par][h]))
                ins.then_inc(q["bda"], 1)
                wait(act, q["st"], p + 1)
                wait(act, q["Yo"], (p - 1) * 4)
                for dst, t in ((bA[par], ast), (bB, bst)):
                    for h, c in halves:
                        ins = nc.scalar.copy(dst[h, :, c], t[h])
                    ins.then_inc(q["bda"], 1)

            def t(j, p, par):
                wait(act, q["tok_mm"], p * 4 + j + 1)
                n = min(4, 15 - 4 * j) * P
                dst = tok[par][:].rearrange("p a b c -> p (a b c)")[:, 4 * j * P:4 * j * P + n]
                nc.scalar.copy(dst, low[:, 0:n]).then_inc(q["tok"], 1)

            def Z(i, p, par):
                if i < LEVELS - 1:
                    wait(act, q["W"], p * 4 + i - 1)
                    wait(act, q["Zc"], p * 5 + i)
                    nc.scalar.copy(zs[:], c3(inv[0][:, 0:TP])).then_inc(q["Zst"], 1)

            def y(_, p, par):
                wait(act, q["done"], p)
                wait(act, q["Yo"], p * 4 + 4)
                nc.scalar.copy(yc[:], y_ps).then_inc(q["Yc"], 1)

            def gv(_, p, par):
                wait(act, q["center"], p + 1)
                nc.scalar.activation(ysq[:], yc[:], ACT.Square).then_inc(q["sqr"], 1)

            def ge(_, p, par):
                wait(act, q["vrecip"], p + 1)
                nc.scalar.activation(rstd[:], rstd[:], ACT.Sqrt).then_inc(q["vsqrt"], 1)

            wait(act, q["zero"], n_zero)
            schedule(act, {"e": e, "lw": lw, "la": la, "lg": lg, "ex": ex, "nm": nm, "ab": ab, "t": t, "Z": Z, "yc": y, "gv": gv, "ge": ge})

        @block.vector
        def _(dve):
            d, n = nc.vector.drain, nc.vector

            def cv(_, p, par):
                d()
                n.tensor_copy(cur[par][:], k.vec[:, :, bass.ds(p, 1)].rearrange("p v a -> p (v a)")).then_inc(q["rm"], 1)

            def e(i, p, par):
                t = (r, kx, v)[i][par][:, PAD + 1:]
                wait(dve, q["own"], p * 3 + i + 1)
                n.tensor_tensor(t, t, tmp[:, 1:T], ALU.add).then_inc(q["shifted"], 1)

            def kn_(_, p, par):
                d()
                n.tensor_scalar(kn[:], kx[par][:], cur[par][:, V_KK:V_KK + 1], None, ALU.mult)
                d()
                n.tensor_tensor(sq[:], kn[:], kn[:], ALU.mult).then_inc(q["ksq"], 1)

            def la(_, p, par):
                wait(dve, q["sig"], p * 3 + 2)
                n.tensor_scalar(sg[:, real], sg[:, real], 0.5, 0.5, ALU.mult, ALU.add)
                n.tensor_scalar(am[:, real], am[:, real], 0.5, -0.5, ALU.mult, ALU.add)
                d()
                n.tensor_tensor_scan(cs[:], k.const[:, C_SCAN:C_SCAN + TP], sg[:], 0.0, ALU.mult, ALU.add)
                n.tensor_scalar(t1[:], am[:], cur[par][:, V_KA:V_KA + 1], 1.0, ALU.mult, ALU.add)
                d()
                n.tensor_tensor(csm[:], cs[:], sg[:], ALU.subtract).then_inc(q["csum"], 1)
                n.tensor_tensor(k2[:], kx[par][:], t1[:], ALU.mult)
                d()
                n.scalar_tensor_tensor(out=rk[:], in0=r[par][:], scalar=cur[par][:, V_RK:V_RK + 1], in1=k2[:],
                                       op0=ALU.mult, op1=ALU.mult).then_inc(q["rk"], 1)

            def nm(_, p, par):
                wait(dve, q["norm"], p + 1)
                n.tensor_scalar(rn[:], low[:, 0:TP], 1e-24, None, ALU.max).then_inc(q["nread"], 1)
                d()
                n.reciprocal(rn[:], rn[:]).then_inc(q["nrecip"], 1)

            def bo(_, p, par):
                wait(dve, q["cpy"], p * 2)
                wait(dve, q["bonus"], p + 1)
                n.tensor_tensor(bon[:], low[:, 0:SEQ], v[par][:, CH:TP], ALU.mult).then_inc(q["bonr"], 1)

            def ab(_, p, par):
                wait(dve, q["exps"], p + 1)
                n.tensor_tensor(rst[par][:], c3(r[par][:]), c3(pe_[:]), ALU.mult)
                for h, c in halves:
                    ins = n.tensor_tensor(bK[h, :, c], c3(k2[h]), c3(pi[h]), ALU.mult)
                ins.then_inc(q["bdv"], 1)
                wait(dve, q["nsqrt"], p + 1)
                n.tensor_tensor(kn[:], kn[:], rn[:], ALU.mult)
                d()
                n.tensor_tensor(ast[:], c3(kn[:]), c3(pm[:]), ALU.mult)
                n.scalar_tensor_tensor(out=k2[:], in0=am[:], scalar=1.0, in1=kn[:], op0=ALU.add, op1=ALU.mult)
                d()
                n.scalar_tensor_tensor(out=bst[:], in0=c3(k2[:]), scalar=-1.0, in1=c3(pi[:]), op0=ALU.mult, op1=ALU.mult).then_inc(q["st"], 1)

            def gr(_, p, par):
                n.tensor_copy(ends[par][:], pe_[:, CH - 1::CH]).then_inc(q["endc"], 1)
                wait(dve, q["gram"], p * 3 + 1)
                n.tensor_tensor(lt[:], c3(inv[0][:, 0:TP]), mask(C_SU, NCH), ALU.mult).then_inc(q["maskT"], 1)
                wait(dve, q["gram"], p * 3 + 2)
                n.tensor_tensor(xt[:], c3(inv[1][:, 0:TP]), mask(C_M1, NCH), ALU.mult).then_inc(q["lread"], 1)
                d()
                n.tensor_tensor(xs[:], xt[:], mask(C_IST, NCH), ALU.add).then_inc(q["X"], 1)
                n.tensor_tensor(ys[:], lt[:], mask(C_LEV, NCH), ALU.mult)
                d()
                n.tensor_tensor(ys[:], ys[:], mask(C_IST, NCH), ALU.add)
                d()
                for h, c in halves:
                    ins = n.tensor_copy(bY[par][h, :, c], ys[h])
                ins.then_inc(q["Y"], 1)

            def rb(_, p, par):
                wait(dve, q["gram2"], p * 2 + 1)
                n.tensor_tensor(rbt[par][:], c3(inv[0][:, 0:SEQ]), mask(C_IU, 4), ALU.mult).then_inc(q["rbr"], 1)

            def rk_(_, p, par):
                wait(dve, q["gram2"], p * 2 + 2)
                n.tensor_tensor(rkt[par][:], c3(inv[1][:, 0:SEQ]), mask(C_IU, 4), ALU.mult).then_inc(q["rbr"], 1)
                for h, c in halves:
                    ins = n.tensor_tensor(bMT[par][h, :, c], c3(inv[2][h, 0:TP]), mask(C_SU, NCH, h), ALU.mult)
                ins.then_inc(q["mtr"], 1)

            def Z(i, p, par):
                wait(dve, q["Z"], p * 5 + i)
                for h, c in halves:
                    ins = n.tensor_copy(bZ[h, :, c], c3(inv[0][h, 0:TP]))
                ins.then_inc(q["Zc"], 1)

            def W_(i, p, par):
                wait(dve, q["WT"], p * 5 + i)
                if i < LEVELS - 1:
                    n.tensor_tensor(ys[:], ys[:], c3(inv[1][:, 0:TP]), ALU.add)
                    wait(dve, q["W"], p * 4 + i)
                    n.tensor_tensor(xs[:], xs[:], c3(inv[2][:, 0:TP]), ALU.add).then_inc(q["X"], 1)
                    d()
                    for h, c in halves:
                        ins = n.tensor_copy(bY[par][h, :, c], ys[h])
                else:
                    for h, c in halves:
                        ins = n.tensor_tensor(bY[par][h, :, c], ys[h], c3(inv[1][h, 0:TP]), ALU.add)
                ins.then_inc(q["Y"], 1)

            def r_(c, p, par):
                wait(dve, q["rhs"], p * 5 + c + 1)
                n.tensor_copy(rhs[:], rhs_ps).then_inc(q["rhsc"], 1)
                if 0 < c < NCH - 1:
                    n.tensor_scalar(spc[:], s[c % 2][:], ends[par][:, c:c + 1], None, ALU.mult)

            def u_(c, p, par):
                wait(dve, q["U"], p * 5 + c + 1)
                n.tensor_copy(u[:], u_ps).then_inc(q["Uc"], 1)

            def s_(c, p, par):
                if c < NCH - 1:
                    d()
                    wait(dve, q["Snew"], p * 4 + c + 1)
                    end, new = ends[par][:, c:c + 1], s[(c + 1) % 2][:]
                    if c:
                        ins = n.scalar_tensor_tensor(out=new, in0=s_ps, scalar=end, in1=spc[:], op0=ALU.mult, op1=ALU.add)
                    else:
                        ins = n.tensor_scalar(new, s_ps, end, None, ALU.mult)
                    ins.then_inc(q["S"], 1)
                    d()

            def gm(_, p, par):
                n.tensor_copy(gcur[:], k.vec[:, V_GNG:V_GNB + 1, bass.ds(p, 1)].rearrange("p v a -> p (v a)"))
                wait(dve, q["mean"], p + 1)
                n.scalar_tensor_tensor(out=yc[:], in0=mean_ps, scalar=-1.0 / HEAD, in1=yc[:], op0=ALU.mult, op1=ALU.add).then_inc(q["center"], 1)

            def gv(_, p, par):
                wait(dve, q["var"], p + 1)
                n.tensor_scalar(rstd[:], var_ps, 1.0 / HEAD, GN_EPS, ALU.mult, ALU.add)
                d()
                n.reciprocal(rstd[:], rstd[:]).then_inc(q["vrecip"], 1)

            def ge(_, p, par):
                wait(dve, q["vsqrt"], p + 1)
                n.tensor_tensor(yc[:], yc[:], rstd[:], ALU.mult)
                d()
                n.tensor_scalar(yc[:], yc[:], gcur[:, 0:1], gcur[:, 1:2], ALU.mult, ALU.add)
                d()
                n.tensor_tensor(yc[:], yc[:], bon3[par][:], ALU.add)
                d()
                n.tensor_tensor(k.yaT[:, bass.ds(p, 1), :].rearrange("p a t -> p (a t)"), yc[:], gate3[par][:], ALU.mult).then_inc(q["done"], 1)

            for t in bY:
                n.memset(t[:], 0.0)
            wait(dve, q["zero"], n_zero)
            schedule(dve, {"cv": cv, "e": e, "kn": kn_, "la": la, "nm": nm, "bo": bo, "ab": ab, "gr": gr, "rb": rb, "rk": rk_,
                           "Z": Z, "W": W_, "r": r_, "u": u_, "s": s_, "gm": gm, "gv": gv, "ge": ge})


def norm_stats(nc, x, n, stats, mv, rs):
    for j in range(4):
        nc.vector.bn_stats(stats[0:n, j, :], x[:, 512 * j:512 * (j + 1)])
    nc.vector.drain()
    nc.vector.bn_aggr(mv[0:n, :], stats[0:n, :, :])
    nc.vector.drain()
    nc.vector.tensor_scalar(rs[0:n, 0:1], mv[0:n, 1:2], LN_EPS, None, ALU.add)
    nc.vector.drain()
    return nc.vector.reciprocal(rs[0:n, 1:2], rs[0:n, 0:1])


def norm_apply(nc, x, n, mv, rs, gamma, beta):
    y, t = rs[0:n, 2:3], rs[0:n, 3:4]
    nc.vector.drain()
    nc.vector.tensor_scalar(t, y, y, rs[0:n, 0:1], ALU.mult, ALU.mult)
    nc.vector.drain()
    nc.vector.tensor_scalar(t, t, -0.5, 1.5, ALU.mult, ALU.add)
    nc.vector.drain()
    nc.vector.tensor_tensor(y, y, t, ALU.mult)
    nc.vector.drain()
    nc.vector.tensor_scalar(x, x, mv[0:n, 0:1], y, ALU.subtract, ALU.mult)
    nc.vector.drain()
    nc.vector.tensor_tensor(x, x, gamma[0:n, :], ALU.mult)
    nc.vector.drain()
    return nc.vector.tensor_tensor(x, x, beta[0:n, :], ALU.add)


def row_broadcast(v):
    return v.rearrange("(a d) -> a d", a=1).to_broadcast((P, D))


def pool_stage(k, w):
    nc = k.nc
    groups, gd = len(POOL_WINDOWS), POOL_DIM // len(POOL_WINDOWS)
    gt = gd // P
    with ExitStack() as ctx:
        wt = [k.sb(f"pool_weights{i}", [P, KT, gd], ctx=ctx) for i in range(2)]
        wm = k.sb("pool_mix", [P, groups, gt, gd], ctx=ctx)
        uu = k.sb("pool_in", [P, 2, gt, T], ctx=ctx)
        sm = k.sb("pool_sums", [P, 2, gt, T], ctx=ctx)
        pd = k.sb("pooled", [P, 2, gt, SEQ], ctx=ctx)
        pu = [[k.ps(f"pool_u{i}{j}", [P, 512], ctx) for j in range(gt)] for i in range(2)]
        pm = [[k.ps(f"pool_m{i}{j}", [P, 512], ctx) for j in range(gt)] for i in range(2)]
        s_w, s_wm = [k.sem("pool_w0"), k.sem("pool_w1")], k.sem("pool_wm")
        s_u, s_uc, s_pd, s_m, s_y = k.sem("pool_u"), k.sem("pool_uc"), k.sem("pool_d"), k.sem("pool_m"), k.sem("pool_y")
        src = w["w_in"][0].rearrange("(k p) c -> p k c", p=P)
        block = ctx.enter_context(nc.Block())

        @block.sync
        def _(sp):
            for g in range(groups):
                wait(sp, s_u, gt * (g - 1))
                sp.dma_start(wt[g % 2][:], src[:, :, POOL0 + g * gd:POOL0 + (g + 1) * gd]).then_inc(s_w[g % 2], 16)
                if g == 0:
                    for h in range(groups):
                        sp.dma_start(wm[:, h, :, :], w["w_pool"][0, h].rearrange("(j p) d -> p j d", p=P)).then_inc(s_wm, 16)

        @block.tensor
        def _(pe):
            def mix(g):
                wait(pe, s_pd, g + 1)
                wait(pe, s_y, gt * (g - 1))
                for j in range(gt):
                    for i in range(gt):
                        mm = nc.tensor.matmul(pm[g % 2][j][:, 0:SEQ], wm[:, g, i, j * P:(j + 1) * P], pd[:, g % 2, i, :],
                                              start=(i == 0), stop=(i == gt - 1))
                    mm.then_inc(s_m, 1)

            pe.wait_ge(s_wm, 16 * groups)
            for g in range(groups):
                wait(pe, s_w[g % 2], 16 * (g // 2 + 1))
                wait(pe, s_uc, gt * (g - 1))
                for j in range(gt):
                    for kt in range(KT):
                        mm = nc.tensor.matmul(pu[g % 2][j][:, 0:T], wt[g % 2][:, kt, j * P:(j + 1) * P], k.hT[:, kt, :],
                                              start=(kt == 0), stop=(kt == KT - 1))
                    mm.then_inc(s_u, 1)
                if g:
                    mix(g - 1)
            mix(groups - 1)

        @block.vector
        def _(dve):
            for g, window in enumerate(POOL_WINDOWS):
                a, b = uu[:, g % 2], sm[:, g % 2]
                dve.wait_ge(s_uc, gt * (g + 1))
                src_, dst, size, c0 = a, b, 1, 0
                nc.vector.tensor_tensor(b[:, :, 1:], a[:, :, 1:], a[:, :, 0:T - 1], ALU.add)
                size, c0 = 2, 1
                while size < window:
                    nc.vector.drain()
                    nc.vector.tensor_tensor(k.pool_tmp[:, :, c0 + size:], b[:, :, c0 + size:], b[:, :, c0:T - size], ALU.add)
                    c0, size = c0 + size, 2 * size
                    nc.vector.drain()
                    nc.vector.tensor_copy(b[:, :, c0:], k.pool_tmp[:, :, c0:])
                nc.vector.drain()
                wait(dve, s_m, gt * (g - 1))
                nc.vector.scalar_tensor_tensor(out=pd[:, g % 2], in0=b[:, :, META:], scalar=1.0 / window, in1=a[:, :, META:],
                                               op0=ALU.mult, op1=ALU.subtract).then_inc(s_pd, 1)

        @block.scalar
        def _(act):
            def out(g):
                for j in range(gt):
                    act.wait_ge(s_m, gt * g + j + 1)
                    m = g * gt + j
                    nc.scalar.activation(k.ybT[:, m, :], pm[g % 2][j][:, 0:SEQ], ACT.Copy, scale=k.pool_scale[:, m:m + 1]).then_inc(s_y, 1)

            for g in range(groups):
                wait(act, s_pd, g - 1)
                for j in range(gt):
                    act.wait_ge(s_u, gt * g + j + 1)
                    nc.scalar.copy(uu[:, g % 2, j, :], pu[g % 2][j][:, 0:T]).then_inc(s_uc, 1)
                if g:
                    out(g - 1)
            out(groups - 1)


def merge_stage(k, w):
    nc = k.nc
    with ExitStack() as ctx:
        wt = [[k.sb(f"merge_{n}{i}", [P, kt, P], ctx=ctx) for n, kt in (("gate0", KT), ("gate1", KT), ("a", KT), ("b", KT // 2))] for i in range(2)]
        gt = [k.sb(f"merge_gates{i}", [P, 2, SEQ], ctx=ctx) for i in range(2)]
        bias = k.sb("merge_bias", [P, 4], ctx=ctx)
        ps = [[k.ps(f"merge_ps{i}{n}", [P, 512], ctx) for n in range(4)] for i in range(2)]
        s_w = [[k.sem(f"merge_w{i}{n}") for n in range(4)] for i in range(2)]
        s_mm = [k.sem(f"merge_mm{i}") for i in range(2)]
        s_gate = [k.sem(f"merge_gate{i}") for i in range(2)]
        s_load = k.sem("merge_load")
        s_bias, s_done = k.sem("merge_bias"), [k.sem(f"merge_done{i}") for i in range(2)]
        W = w["w_in"][0].rearrange("(k p) c -> p k c", p=P)
        A = w["w_branch_a"][0].rearrange("(k p) c -> p k c", p=P)
        B = w["w_branch_b"][0].rearrange("(k p) c -> p k c", p=P)
        STEPS = KT // 2
        block = ctx.enter_context(nc.Block())

        @block.sync
        def _(sp):
            def load(m, first=False):
                col = 0 if first else sp.snap(m * (2 * P))
                for i in range(2):
                    for n, (src, c0) in enumerate(((W, GATE0), (W, GATE0 + D), (A, 0), (B, 0))):
                        if not first:
                            wait(sp, s_mm[i], m * 4 - 3 + n)
                            sp.sem_inc(s_load, 1)
                        sp.dma_start(wt[i][n][:], src[:, :, bass.ds(col + (c0 + i * P), P)]).then_inc(s_w[i][n], 16)

            load(0, True)
            with sp.Fori(1, STEPS) as m:
                load(m)

        @block.tensor
        def _(pe):
            def step(m, first=False):
                for i in range(2):
                    if not first:
                        wait(pe, s_done[i], m)
                    for n, (rhs, kts) in enumerate(((k.hT[:, :, META:T], KT), (k.hT[:, :, META:T], KT), (k.yaT, KT), (k.ybT, KT // 2))):
                        wait(pe, s_w[i][n], m * 16 + 16)
                        for kt in range(kts):
                            mm = nc.tensor.matmul(ps[i][n][:, 0:SEQ], wt[i][n][:, kt, :], rhs[:, kt, :], start=(kt == 0), stop=(kt == kts - 1))
                        mm.then_inc(s_mm[i], 1)

            step(0, True)
            with pe.Fori(1, STEPS) as m:
                step(m)

        @block.scalar
        def _(act):
            def step(m, first=False):
                wait(act, s_bias, m + 1)
                for i in range(2):
                    for n in range(2):
                        wait(act, s_mm[i], m * 4 + n + 1)
                        nc.scalar.activation(gt[i][:, n, :], ps[i][n][:, 0:SEQ], ACT.Sigmoid, bias=bias[:, 2 * n + i:2 * n + i + 1]).then_inc(s_gate[i], 1)

            step(0, True)
            with act.Fori(1, STEPS) as m:
                step(m)

        @block.vector
        def _(dve):
            def step(m, first=False):
                nc.vector.drain()
                if not first:
                    wait(dve, s_gate[1], m * 2)
                nc.vector.tensor_copy(bias[:].rearrange("p (v a) -> p v a", v=2), k.vec[:, V_BG0:V_BG1 + 1, bass.ds(m * 2, 2)]).then_inc(s_bias, 1)
                for i in range(2):
                    wait(dve, s_gate[i], m * 2 + 2)
                    for n in range(2):
                        wait(dve, s_mm[i], m * 4 + 3 + n)
                        nc.vector.tensor_tensor(gt[i][:, n, :], gt[i][:, n, :], ps[i][2 + n][:, 0:SEQ], ALU.mult)
                    nc.vector.drain()
                    nc.vector.tensor_tensor(k.mT[:, bass.ds(m * 2 + i, 1), :].rearrange("p a t -> p (a t)"), gt[i][:, 0, :], gt[i][:, 1, :], ALU.add).then_inc(s_done[i], 1)

            step(0, True)
            with dve.Fori(1, STEPS) as m:
                step(m)


def out_stage(k, w):
    nc = k.nc
    NB = D // 512
    with ExitStack() as ctx:
        wt = [k.sb(f"out_w{i}", [P, KT, 512], ctx=ctx) for i in range(2)]
        gam, bet = k.sb("ln1_gamma", [P, D], ctx=ctx), k.sb("ln1_beta", [P, D], ctx=ctx)
        stats, mv, rs = k.sb("ln1_stats", [P, TT, 4, 6], ctx=ctx), k.sb("ln1_mv", [P, TT, 2], ctx=ctx), k.sb("ln1_rs", [P, TT, 4], ctx=ctx)
        ps = [[k.ps(f"out_ps{i}{t}", [P, 512], ctx) for t in range(TT)] for i in range(2)]
        tp = [k.ps(f"out_turn{i}", [P, 512], ctx) for i in range(4)]
        s_w, s_gb = [k.sem("out_w0"), k.sem("out_w1")], k.sem("out_gb")
        s_mm = [k.sem("out_mm0"), k.sem("out_mm1")]
        s_ev = [k.sem("out_ev0"), k.sem("out_ev1")]
        s_var, s_rt, s_h, s_tp, s_tc = k.sem("ln1_var"), k.sem("ln1_root"), k.sem("ln1_h"), k.sem("ln1_turn"), k.sem("ln1_turned")
        W = w["w_out"][0].rearrange("(k p) c -> p k c", p=P)
        ident = k.const[:, C_ID:C_ID + P]
        block = ctx.enter_context(nc.Block())

        @block.sync
        def _(sp):
            for n in range(NB):
                wait(sp, s_mm[n % 2], TT * (n // 2))
                sp.dma_start(wt[n % 2][:], W[:, :, n * 512:(n + 1) * 512]).then_inc(s_w[n % 2], 16)
            sp.dma_start(gam[:], row_broadcast(w["ln1_g"][0])).then_inc(s_gb, 16)
            sp.dma_start(bet[:], row_broadcast(w["ln1_b"][0])).then_inc(s_gb, 16)

        @block.tensor
        def _(pe):
            def step(m, first=False):
                for i in range(2):
                    wait(pe, s_w[i], m * 16 + 16)
                    if not first:
                        wait(pe, s_ev[i], m * TT)
                    for t in range(TT):
                        for kt in range(KT):
                            mm = nc.tensor.matmul(ps[i][t][:], k.mT[:, kt, t * P:(t + 1) * P], wt[i][:, kt, :], start=(kt == 0), stop=(kt == KT - 1))
                        mm.then_inc(s_mm[i], 1)

            step(0, True)
            with pe.Fori(1, NB // 2) as m:
                step(m)
            for t in range(TT):
                pe.wait_ge(s_h, t + 1)
                for q4 in range(4):
                    n = t * 4 + q4
                    wait(pe, s_tc, n - 3)
                    for j in range(4):
                        mm = nc.tensor.transpose(tp[q4][:, j * P:(j + 1) * P], k.h[:, t, (4 * q4 + j) * P:(4 * q4 + j + 1) * P], ident)
                    mm.then_inc(s_tp, 1)

        @block.vector
        def _(dve):
            def step(m):
                for i in range(2):
                    for t in range(TT):
                        wait(dve, s_mm[i], m * TT + t + 1)
                        x = k.h[:, t, bass.ds(m * 1024 + i * 512, 512)]
                        nc.vector.scalar_tensor_tensor(out=x, in0=x, scalar=ALPHA, in1=ps[i][t][:], op0=ALU.mult, op1=ALU.add).then_inc(s_ev[i], 1)

            step(0)
            with dve.Fori(1, NB // 2) as m:
                step(m)
            nc.vector.drain()
            for t in range(TT):
                norm_stats(nc, k.h[:, t, :], P, stats[:, t], mv[:, t], rs[:, t]).then_inc(s_var, 1)
            dve.wait_ge(s_gb, 32)
            for t in range(TT):
                dve.wait_ge(s_rt, t + 1)
                norm_apply(nc, k.h[:, t, :], P, mv[:, t], rs[:, t], gam, bet).then_inc(s_h, 1)

        @block.scalar
        def _(act):
            for t in range(TT):
                act.wait_ge(s_var, t + 1)
                nc.scalar.activation(rs[:, t, 2:3], rs[:, t, 1:2], ACT.Sqrt).then_inc(s_rt, 1)
            for t in range(TT):
                for q4 in range(4):
                    act.wait_ge(s_tp, t * 4 + q4 + 1)
                    nc.scalar.copy(k.h1T[:, 4 * q4:4 * q4 + 4, t * P:(t + 1) * P], tp[q4][:].rearrange("p (j t) -> p j t", t=P)).then_inc(s_tc, 1)


def router_stage(k, w):
    nc = k.nc
    NEG = -3.0e38
    with ExitStack() as ctx:
        sb = lambda name, shape, dt=F32: k.sb(name, shape, dt, ctx=ctx)
        wt = [[sb(f"query_w{j}{i}", [P, KT, P]) for i in range(2)] for j in range(2)]
        keys, kT = sb("keys", [P, 2, P]), sb("keysT", [P, 2, P])
        qT = [sb(f"queryT{i}", [P, SEQ]) for i in range(2)]
        sc, sc2 = sb("scores", [P, TT, 2, N_KEYS]), sb("scores_left", [P, TT, 2, N_KEYS])
        sv, si = sb("side_best", [P, TT, 2, TOPK]), sb("side_index", [P, TT, 2, TOPK], U32)
        sif = sb("side_index_f", [P, TT, 2, TOPK])
        cand, cand2 = sb("candidates", [P, TT, TOPK, TOPK]), sb("candidates_left", [P, TT, TOPK * TOPK])
        tv, ti = sb("top", [P, TT, TOPK]), sb("top_pos", [P, TT, TOPK], U32)
        pij, pf = sb("top_side_pos", [P, 2, TT, TOPK], U32), sb("top_side_pos_f", [P, 2, TT, TOPK])
        hot = sb("one_hot", [P, 2, TT * TOPK, TOPK])
        ef, ex = sb("expert_sides", [P, 2, TT, TOPK]), sb("expert_f", [P, TT, TOPK])
        mx, ss = sb("gate_sum", [P, TT, HEADS]), sb("gate_rsum", [P, TT, HEADS])
        pq = [k.ps(f"query_ps{i}", [P, 512], ctx) for i in range(2)]
        pk = [k.ps(f"score_ps{i}", [P, 512], ctx) for i in range(2)]
        pt = k.ps("keys_turn", [P, 512], ctx)
        names = ("key_in", "key_turn", "key", "q_mm", "q", "s_mm", "s", "scored", "found", "exp", "shift", "seen")
        s = {n: k.sem(f"route_{n}") for n in names}
        s_w = [[k.sem(f"route_w{j}{i}") for i in range(2)] for j in range(2)]
        W = w["w_q_peer"][0].rearrange("(k p) c -> p k c", p=P)
        ident = k.const[:, C_ID:C_ID + P]
        iota = k.const[:, C_IOTA:C_IOTA + TOPK]
        block = ctx.enter_context(nc.Block())

        @block.sync
        def _(sp):
            sp.dma_start(keys[:], w["sub_keys"][0].rearrange("s k c -> k s c")).then_inc(s["key_in"], 16)

            def load(m, first=False):
                col = sp.snap(m * (4 * P)) if not first else 0
                for j in range(2):
                    for i in range(2):
                        if not first:
                            wait(sp, s["q_mm"], m * 4 - 3 + 2 * j + i)
                        sp.dma_start(wt[j][i][:], W[:, :, bass.ds(col + (2 * j + i) * P, P)]).then_inc(s_w[j][i], 16)

            load(0, True)
            with sp.Fori(1, HEADS // 2) as m:
                load(m)

        @block.tensor
        def _(pe):
            pe.wait_ge(s["key_in"], 16)
            for i in range(2):
                mm = nc.tensor.transpose(pt[:, i * P:(i + 1) * P], keys[:, i, :], ident)
            mm.then_inc(s["key_turn"], 1)
            pe.wait_ge(s["key"], 1)

            def step(m, first=False):
                for j in range(2):
                    for i in range(2):
                        wait(pe, s_w[j][i], m * 16 + 16)
                        if not (first and j == 0):
                            wait(pe, s["q"], m * 4 + 2 * j - 1 + i)
                        for kt in range(KT):
                            mm = nc.tensor.matmul(pq[i][:, 0:SEQ], wt[j][i][:, kt, :], k.h1T[:, kt, :], start=(kt == 0), stop=(kt == KT - 1))
                        mm.then_inc(s["q_mm"], 1)
                    for i in range(2):
                        wait(pe, s["q"], m * 4 + 2 * j + i + 1)
                        if not (first and j == 0):
                            wait(pe, s["s"], m * 4 + 2 * j - 1 + i)
                        for t in range(TT):
                            mm = nc.tensor.matmul(pk[i][:, t * P:(t + 1) * P], qT[i][:, t * P:(t + 1) * P], kT[:, i, :], start=True, stop=True)
                        mm.then_inc(s["s_mm"], 1)

            step(0, True)
            with pe.Fori(1, HEADS // 2) as m:
                step(m)

        @block.scalar
        def _(act):
            act.wait_ge(s["key_turn"], 1)
            nc.scalar.copy(kT[:], pt[:, 0:2 * P].rearrange("p (s c) -> p s c", s=2)).then_inc(s["key"], 1)

            def step(m, first=False):
                for j in range(2):
                    for i in range(2):
                        wait(act, s["q_mm"], m * 4 + 2 * j + i + 1)
                        if not (first and j == 0):
                            wait(act, s["s_mm"], m * 4 + 2 * j + i - 1)
                        nc.scalar.copy(qT[i][:], pq[i][:, 0:SEQ]).then_inc(s["q"], 1)
                    for i in range(2):
                        wait(act, s["s_mm"], m * 4 + 2 * j + i + 1)
                        if not (first and j == 0):
                            wait(act, s["scored"], m * 2 + j)
                        nc.scalar.copy(sc[:, :, i, :], pk[i][:, 0:TT * P].rearrange("p (t k) -> p t k", t=TT)).then_inc(s["s"], 1)

            step(0, True)
            with act.Fori(1, HEADS // 2) as m:
                step(m)
            act.wait_ge(s["shift"], 1)
            nc.scalar.activation(k.gates[:], k.gates[:], ACT.Exp).then_inc(s["exp"], 1)

        @block.vector
        def _(dve):
            v, d = nc.vector, nc.vector.drain

            def best16(value, index, values, left, where):
                for o in where:
                    v.max(value(o)[:, 0:8], values(o))
                d()
                for o in where:
                    v.max_index(index(o)[:, 0:8], value(o)[:, 0:8], values(o))
                    ins = v.match_replace(left(o), value(o)[:, 0:8], values(o), NEG)
                d()
                for o in where:
                    v.max(value(o)[:, 8:16], left(o))
                d()
                for o in where:
                    v.max_index(index(o)[:, 8:16], value(o)[:, 8:16], left(o))
                return ins

            def step(m, j):
                wait(dve, s["s"], m * 4 + 2 * j + 2)
                dve.sem_inc(s["seen"], 1)
                sides = [(t, i) for t in range(TT) for i in range(2)]
                best16(lambda o: sv[:, o[0], o[1], :], lambda o: si[:, o[0], o[1], :], lambda o: sc[:, o[0], o[1], :],
                       lambda o: sc2[:, o[0], o[1], :], sides)
                d()
                v.tensor_copy(sif[:], si[:]).then_inc(s["scored"], 1)
                for t in range(TT):
                    v.tensor_tensor(cand[:, t], sv[:, t, 0, :].rearrange("p (a b) -> p a b", b=1).to_broadcast((P, TOPK, TOPK)),
                                    sv[:, t, 1, :].rearrange("p (a b) -> p a b", a=1).to_broadcast((P, TOPK, TOPK)), ALU.add)
                d()
                best16(lambda t: tv[:, t], lambda t: ti[:, t], lambda t: cand[:, t].rearrange("p a b -> p (a b)"), lambda t: cand2[:, t], range(TT))
                d()
                v.tensor_copy(k.gates[:, :, bass.ds(m * 2 + j, 1), :].rearrange("p t a n -> p t (a n)"), tv[:])
                v.tensor_scalar(pij[:, 0], ti[:], 4, None, ALU.logical_shift_right)
                v.tensor_scalar(pij[:, 1], ti[:], 15, None, ALU.bitwise_and)
                d()
                v.tensor_copy(pf[:], pij[:])
                d()
                for i in range(2):
                    v.tensor_tensor(hot[:, i], pf[:, i].rearrange("p t (n a) -> p (t n) a", a=1).to_broadcast((P, TT * TOPK, TOPK)),
                                    iota.rearrange("p (a n) -> p a n", a=1).to_broadcast((P, TT * TOPK, TOPK)), ALU.is_equal)
                d()
                for i in range(2):
                    for t in range(TT):
                        h = hot[:, i, t * TOPK:(t + 1) * TOPK, :]
                        v.tensor_tensor(h, h, sif[:, t, i, :].rearrange("p (a n) -> p a n", a=1).to_broadcast((P, TOPK, TOPK)), ALU.mult)
                d()
                v.tensor_reduce(ef[:].rearrange("p i t n -> p (i t n)"), hot[:].rearrange("p i n c -> p (i n) c"), AX.X, ALU.add)
                d()
                v.scalar_tensor_tensor(out=ex[:], in0=ef[:, 0], scalar=float(N_KEYS), in1=ef[:, 1], op0=ALU.mult, op1=ALU.add)
                d()
                v.tensor_copy(k.idx[:, :, bass.ds(m * 2 + j, 1), :].rearrange("p t a n -> p t (a n)"), ex[:])
                d()

            def steps(m):
                for j in range(2):
                    step(m, j)

            steps(0)
            with dve.Fori(1, HEADS // 2) as m:
                steps(m)
            g = k.gates[:].rearrange("p t h n -> p (t h) n")
            flat = lambda x: x[:].rearrange("p t h -> p (t h)")
            v.tensor_copy(flat(mx), g[:, :, 0])
            d()
            wide = lambda x: x[:].rearrange("p t (h n) -> p (t h) n", n=1).to_broadcast((P, TT * HEADS, TOPK))
            v.tensor_tensor(g, g, wide(mx), ALU.subtract).then_inc(s["shift"], 1)
            dve.wait_ge(s["exp"], 1)
            v.tensor_reduce(flat(mx), g, AX.X, ALU.add)
            d()
            v.reciprocal(flat(ss), flat(mx))
            d()
            v.tensor_tensor(g, g, wide(ss), ALU.mult)


def peer_stage(k, w, out):
    nc = k.nc
    GROUPS = TT * HEADS
    RU, RV, RD = 4, 4, 4
    with ExitStack() as ctx:
        sb = lambda name, shape, dt=F32: k.sb(name, shape, dt, ctx=ctx)
        ur = [sb(f"up_rows{i}", [P, D]) for i in range(RU)]
        vr = [sb(f"down_rows{i}", [P, D]) for i in range(RV)]
        dg = [sb(f"diagonal{i}", [P, P]) for i in range(RD)]
        iu = [sb(f"up_experts{i}", [P, TOPK], I32) for i in range(2)]
        iv = [sb(f"down_experts{i}", [P, TOPK], I32) for i in range(2)]
        gat = [sb(f"group_gates{i}", [P, TOPK]) for i in range(2)]
        dots = [sb(f"dots{i}", [P, TOPK]) for i in range(2)]
        act_ = [sb(f"weights{i}", [P, TOPK]) for i in range(2)]
        aid = sb("alpha_identity", [P, P])
        gam, bet = sb("ln2_gamma", [P, D]), sb("ln2_beta", [P, D])
        y = sb("ln2_y", [P, D])
        stats, mv, rs = sb("ln2_stats", [P, 4, 6]), sb("ln2_mv", [P, 2]), sb("ln2_rs", [P, 4])
        ps = [[k.ps(f"peer_ps{t}{n}", [P, 512], ctx) for n in range(4)] for t in range(TT)]
        s_u = [k.sem(f"up_arrived{i}") for i in range(RU)]
        s_v = [k.sem(f"down_arrived{i}") for i in range(RV)]
        names = ("gather", "idx_u", "idx_v", "dot", "gelu", "weight", "diag", "added", "aid", "gb", "y", "var", "root", "norm", "out", "gate")
        s = {n: k.sem(f"peer_{n}") for n in names}
        ident = k.const[:, C_ID:C_ID + P]
        block = ctx.enter_context(nc.Block())

        def schedule(eng, step):
            step(0, 0, 0, None)
            step(1, 1, 0, 0)
            with eng.Fori(1, HEADS // 2) as m:
                step(m * 2, 0, 0, 0)
                step(m * 2 + 1, 1, 0, 0)
            step(8, 0, 1, 0)
            with eng.Fori(0, 3) as m:
                step(m * 2 + 9, 1, 1, 1)
                step(m * 2 + 10, 0, 1, 1)
            step(15, 1, 1, 1)
            step(16, 0, None, 1)

        @block.sync
        def _(sp):
            sp.dma_start(gam[:], row_broadcast(w["ln2_g"][0])).then_inc(s["gb"], 16)
            sp.dma_start(bet[:], row_broadcast(w["ln2_b"][0])).then_inc(s["gb"], 16)
            for t in range(TT):
                sp.wait_ge(s["norm"], t + 1)
                sp.dma_start(out[0, t * P:(t + 1) * P, :], y[:]).then_inc(s["out"], 16)
            sp.wait_ge(s["out"], 16 * TT)

        @block.gpsimd
        def _(pool):
            def gather(rows, table, ix, j, arrived):
                pool.sem_inc(s["gather"], 1)
                pool.indirect_dma_start(rows[:], None, table, bass.IndirectOffsetOnAxis(ap=ix[:, j:j + 1], axis=0)).then_inc(arrived, 16)

            def step(g, par, tu, tv):
                flat = k.idx[:].rearrange("p t h n -> p (t h) n")
                if tu is not None:
                    nc.gpsimd.tensor_copy(iu[par][:], flat[:, bass.ds(g, 1), :].rearrange("p a n -> p (a n)")).then_inc(s["idx_u"], 1)
                if tv is not None:
                    nc.gpsimd.tensor_copy(iv[par][:], flat[:, bass.ds(g - 1, 1), :].rearrange("p a n -> p (a n)")).then_inc(s["idx_v"], 1)
                if tu is not None:
                    wait(pool, s["idx_u"], g + 1)
                if tv is not None:
                    wait(pool, s["idx_v"], g)
                for j in range(TOPK):
                    if tu is not None:
                        if not isinstance(g, int) or g * TOPK + j >= RU:
                            wait(pool, s["dot"], g * TOPK + (j - RU + 1))
                        gather(ur[j % RU], w["u_table"][0], iu[par], j, s_u[j % RU])
                    if tv is not None:
                        if not isinstance(g, int) or (g - 1) * TOPK + j >= RV:
                            wait(pool, s["added"], (g - 1) * TOPK + (j - RV + 1))
                        gather(vr[j % RV], w["v_table"][0], iv[par], j, s_v[j % RV])

            schedule(pool, step)

        @block.vector
        def _(dve):
            v, d = nc.vector, nc.vector.drain
            v.tensor_scalar(aid[:], ident, ALPHA, None, ALU.mult).then_inc(s["aid"], 1)

            def finish(t):
                if t:
                    dve.wait_ge(s["out"], 16 * t)
                for n in range(4):
                    v.tensor_copy(y[:, n * 512:(n + 1) * 512], ps[t][n][:])
                d()
                norm_stats(nc, y[:, :], P, stats, mv, rs).then_inc(s["var"], 1)
                dve.wait_ge(s["root"], t + 1)
                norm_apply(nc, y[:, :], P, mv, rs, gam, bet).then_inc(s["norm"], 1)

            def step(g, par, tu, tv):
                if tu is not None:
                    if not isinstance(g, int) or g >= 2:
                        wait(dve, s["diag"], (g - 1) * TOPK)
                    x = k.gates[:].rearrange("p t h n -> p (t h) n")[:, bass.ds(g, 1), :].rearrange("p a n -> p (a n)")
                    v.tensor_copy(gat[par][:], x).then_inc(s["gate"], 1)
                    for j in range(TOPK):
                        wait(dve, s_u[j % RU], g * (16 * TOPK // RU) + 16 * (j // RU + 1))
                        v.tensor_tensor_reduce(ur[j % RU][:], ur[j % RU][:], k.h[:, tu, :], 1.0, 0.0, ALU.mult, ALU.add,
                                               dots[par][:, j:j + 1]).then_inc(s["dot"], 1)
                    wait(dve, s["gelu"], g + 1)
                    v.tensor_tensor(act_[par][:], dots[par][:], gat[par][:], ALU.mult).then_inc(s["weight"], 1)
                if isinstance(g, int) and g in (HEADS, GROUPS):
                    wait(dve, s["added"], g * TOPK)
                    if g == HEADS:
                        dve.wait_ge(s["gb"], 32)
                    finish(g // HEADS - 1)

            schedule(dve, step)

        @block.scalar
        def _(act):
            def step(g, par, tu, tv):
                if tv is not None:
                    wait(act, s["weight"], g)
                    for j in range(TOPK):
                        if not isinstance(g, int) or (g - 1) * TOPK + j >= RD:
                            wait(act, s["added"], (g - 1) * TOPK + (j - RD + 1))
                        nc.scalar.activation(dg[j % RD][:], ident, ACT.Copy, scale=act_[1 - par][:, j:j + 1]).then_inc(s["diag"], 1)
                if tu is not None:
                    wait(act, s["dot"], g * TOPK + TOPK)
                    nc.scalar.activation(dots[par][:], dots[par][:], ACT.Gelu).then_inc(s["gelu"], 1)
                if isinstance(g, int) and g in (HEADS, GROUPS):
                    act.wait_ge(s["var"], g // HEADS)
                    nc.scalar.activation(rs[:, 2:3], rs[:, 1:2], ACT.Sqrt).then_inc(s["root"], 1)

            schedule(act, step)

        @block.tensor
        def _(pe):
            pe.wait_ge(s["aid"], 1)
            for t in range(TT):
                for n in range(4):
                    nc.tensor.matmul(ps[t][n][:], aid[:], k.h[:, t, n * 512:(n + 1) * 512], start=True, stop=False, skip_group_check=True)

            def step(g, par, tu, tv):
                if tv is None:
                    return
                last = isinstance(g, int) and g in (HEADS, GROUPS)
                for j in range(TOPK):
                    wait(pe, s_v[j % RV], (g - 1) * (16 * TOPK // RV) + 16 * (j // RV + 1))
                    wait(pe, s["diag"], (g - 1) * TOPK + j + 1)
                    for n in range(4):
                        mm = nc.tensor.matmul(ps[tv][n][:], dg[j % RD][:], vr[j % RV][:, n * 512:(n + 1) * 512], start=False,
                                              stop=(last and j == TOPK - 1), skip_group_check=True)
                    mm.then_inc(s["added"], 1)

            schedule(pe, step)


def program(nc, w, out):
    ctx = ExitStack()
    with ctx:
        k = Core(nc, ctx)
        k.lora_tiles = ((LORA0, DECAY_LORA), (LORA0 + DECAY_LORA, ICL_LORA),
                        (POOL0 - GATE_LORA, P), (POOL0 - P, P))
        k.const = k.sb("constants", [P, NCONST])
        k.h = k.sb("h", [P, TT, D])
        k.vec = k.sb("vectors", [P, NVEC, PAIRS])
        k.pool_scale = k.sb("pool_scale_t", [P, POOL_DIM // P])
        k.mu_lora = k.sb("mu_lora", [P, 4])
        k.om_lora = k.sb("one_minus_mu_lora", [P, 4])
        k.idx = k.sb("experts", [P, TT, HEADS, TOPK], I32)
        k.gates = k.sb("gates", [P, TT, HEADS, TOPK])
        with ExitStack() as front:
            k.yaT = k.sb("yaT", [P, KT, SEQ], ctx=front)
            k.hT = k.sb("hT", [P, KT, T], ctx=front)
            k.lora = k.sb("lora", [P, 4, T], ctx=front)
            input_stage(k, w)
            lora_stage(k, w)
            rwkv_stage(k, w)
            k.ybT = k.sb("ybT", [P, KT // 2, SEQ], ctx=front)
            k.pool_tmp = k.sb("pool_tmp", [P, 2, T], ctx=front)
            pool_stage(k, w)
            k.mT = k.sb("mergedT", [P, KT, SEQ], ctx=front)
            merge_stage(k, w)
            k.h1T = k.sb("h1T", [P, KT, SEQ], ctx=front)
            out_stage(k, w)
            router_stage(k, w)
        peer_stage(k, w, out)



_INS = ["x", "meta_tokens", "ln_in_g", "ln_in_b", "w_in", "mu_shift", "w0", "w_w2", "a0", "w_a2", "w_g2", "k_k", "k_a", "r_k",
        "gn_g", "gn_b", "w_pool", "pool_scale", "b_gate", "w_branch_a", "w_branch_b", "w_out", "ln1_g", "ln1_b", "w_q_peer",
        "sub_keys", "u_table", "v_table", "ln2_g", "ln2_b"]


def kernel(**inputs):
    import numpy as _np
    import concourse.bacc as _bacc
    from concourse import mybir as _mybir
    from concourse.bass_utils import run_bass_kernel_spmd as _run

    nc = _bacc.Bacc("TRN2", target_bir_lowering=False, num_devices=1)
    arrays = {f"in_{n}": _np.ascontiguousarray(inputs[n]) for n in _INS}
    arrays["in_consts"] = constants()
    w = {n[3:]: nc.dram_tensor(n, a.shape, _mybir.dt.from_np(a.dtype), kind="ExternalInput").ap() for n, a in arrays.items()}
    out = nc.dram_tensor("out", (1, SEQ, D), F32, kind="ExternalOutput").ap()
    program(nc, w, out)
    r = _run(nc, [arrays], core_ids=[0])
    return r.results[0]["out"]
```

```python
import concourse.bass as bass
from concourse import mybir
from contextlib import ExitStack
import numpy as np

F32 = mybir.dt.float32
I32 = mybir.dt.int32
U32 = mybir.dt.uint32
F32R = mybir.dt.float32r
ALU = mybir.AluOpType
ACT = mybir.ActivationFunctionType
AX = mybir.AxisListType

P = 128
D = 2048
KT = D // P
META = 16
SEQ = 256
T = META + SEQ
TT = SEQ // P
HEAD = 64
PAIRS = D // P
CH = 64
NCH = 5
TP = NCH * CH
PAD = TP - T
DECAY_LORA = ICL_LORA = 96
GATE_LORA = 256
DECAY = float(np.exp(-0.5))
GN_EPS = 64e-5
LN_EPS = 1e-5
LORA0 = 3 * D
POOL0 = LORA0 + DECAY_LORA + ICL_LORA + GATE_LORA
POOL_DIM = D // 2
POOL_WINDOWS = (2, 4, 8, 16)
GATE0 = POOL0 + POOL_DIM
HEADS = 8
TOPK = 16
N_KEYS = 128
ALPHA = 2.0 ** 0.25
LEVELS = 6

C_ID, C_ONES, C_SCAN, C_SU, C_IU, C_M1, C_IST = 0, 128, 256, 576, 640, 704, 768
C_LEV = 832
C_IOTA = C_LEV + 64 * (LEVELS - 1 + 1)
NCONST = C_IOTA + 16


def constants():
    c = np.zeros((P, NCONST), np.float32)
    p, s = np.arange(P)[:, None], np.arange(P)[:, None] % CH
    c[:, C_ID:C_ID + P] = np.eye(P)
    c[:, C_ONES:C_ONES + P] = p // HEAD == np.arange(P)[None] // HEAD
    c[:, C_SCAN:C_SCAN + TP] = np.arange(TP)[None] % CH != 0
    t = np.arange(CH)[None]
    c[:, C_SU:C_SU + CH] = s < t
    c[:, C_IU:C_IU + CH] = s <= t
    c[:, C_M1:C_M1 + CH] = (s % 2 == 1) & (t == s - 1)
    c[:, C_IST:C_IST + CH] = s == t
    for i in range(LEVELS):
        b = 1 << i
        c[:, C_LEV + CH * i:C_LEV + CH * (i + 1)] = (t // b % 2 == 1) & (s // b == t // b - 1)
    c[:, C_IOTA:C_IOTA + 16] = np.arange(16)[None]
    return c


(V_MUR, V_MUK, V_MUV, V_W0, V_A0, V_KK, V_KA, V_RK, V_GNG, V_GNB, V_BG0, V_BG1,
 V_OMR, V_OMK, V_OMV, V_W0H, V_A0H) = range(17)
NRAW, NVEC = 12, 17


class Core:

    def __init__(self, nc, ctx):
        self.nc, self.ctx, self.sems = nc, ctx, []

    def sem(self, name):
        s = self.nc.alloc_semaphore(name)
        self.sems.append(s)
        return s

    def release_sems(self):
        self.nc.clear_and_free_semaphores(self.sems)
        self.nc.all_engine_barrier()
        self.sems = []

    def sb(self, name, shape, dt=F32, ctx=None):
        return (ctx or self.ctx).enter_context(self.nc.sbuf_tensor(name, shape, dt))

    def ps(self, name, shape, ctx):
        return ctx.enter_context(self.nc.psum_tensor(name, shape, F32))


def wait(eng, sem, value):
    if not isinstance(value, int) or value > 0:
        eng.wait_ge(sem, value)


def leading_bits(nc, high, x):
    return nc.vector.tensor_copy(high.bitcast(F32R), x)


def rest_bits(eng, low, x, high):
    return eng.tensor_tensor(low.bitcast(F32R), x, high, ALU.subtract)


def split(nc, high, low, x):
    leading_bits(nc, high, x)
    nc.vector.drain()
    return rest_bits(nc.vector, low, x, high)


def product(nc, out, wts, x, start, stop):
    (wh, wl), (xh, xl) = wts, x
    for n, (a, b) in enumerate(((wh, xh), (wh, xl), (wl, xh))):
        mm = nc.tensor.matmul(out, a.bitcast(F32R), b.bitcast(F32R), start=start and n == 0, stop=stop and n == 2)
    return mm


def input_stage(k, w):
    nc = k.nc
    with ExitStack() as ctx:
        xm = k.sb("x_meta", [META, D], ctx=ctx)
        gam = k.sb("ln_in_gamma", [P, D], ctx=ctx)
        bet = k.sb("ln_in_beta", [P, D], ctx=ctx)
        raw = k.sb("raw_vectors", [P, 2, P], ctx=ctx)
        stats = k.sb("ln_stats", [P, 3, 4, 6], ctx=ctx)
        mv = k.sb("ln_mean_var", [P, 3, 2], ctx=ctx)
        rs = k.sb("ln_rstd", [P, 3, 2], ctx=ctx)
        tp = [k.ps(f"turn{i}", [P, 512], ctx) for i in range(4)]
        pv = k.ps("turn_vectors", [P, 256], ctx)
        s_zero, s_rest = k.sem("in_zero"), k.sem("in_rest")
        s_x0, s_const, s_x, s_raw = k.sem("in_x0"), k.sem("in_const"), k.sem("in_x"), k.sem("in_raw")
        s_gb, s_var, s_rstd, s_h = k.sem("in_gamma_beta"), k.sem("in_var"), k.sem("in_rstd"), k.sem("in_h")
        s_turn, s_out, s_pv = k.sem("in_turned"), k.sem("in_evacuated"), k.sem("in_vectors_turned")
        ident = k.const[:, C_ID:C_ID + P]
        tiles = [(xm[:, :], META, 0), (k.h[:, 0, :], P, META), (k.h[:, 1, :], P, META + P)]
        block = ctx.enter_context(nc.Block())

        @block.sync
        def _(sp):
            sp.dma_start(k.h[:, 0, :], w["x"][0, 0:P, :]).then_inc(s_x0, 16)
            sp.dma_start(k.h[:, 1, :], w["x"][0, P:SEQ, :]).then_inc(s_x, 16)
            sp.dma_start(xm[:], w["meta_tokens"]).then_inc(s_x, 16)
            sp.dma_start(gam[:], w["ln_in_g"].rearrange("(a d) -> a d", a=1).to_broadcast((P, D))).then_inc(s_gb, 16)
            sp.dma_start(bet[:], w["ln_in_b"].rearrange("(a d) -> a d", a=1).to_broadcast((P, D))).then_inc(s_gb, 16)
            sp.dma_start(k.const[:], w["consts"]).then_inc(s_const, 16)
            src = w["w_in"][0].rearrange("(k p) c -> p k c", p=P)
            for g in range(4):
                sp.dma_start(k.lora_raw[:, 4 * g:4 * g + 4, :], src[:, 4 * g:4 * g + 4, LORA0:POOL0]).then_inc(k.s_lora_w[g], 16)

        @block.gpsimd
        def _(pool):
            mu = w["mu_shift"][0, 0:3 * D].rearrange("(r c) -> r c", c=P)
            nc.gpsimd.memset(raw[:], 0.0).then_inc(s_zero, 1)
            nc.gpsimd.memset(k.mu_lora[:], 0.0).then_inc(s_zero, 1)
            pool.wait_ge(s_zero, 2)
            rows = [mu] + [w[n][0].rearrange("(r c) -> r c", c=P) for n in ("w0", "a0", "k_k", "k_a")]
            rows += [w["r_k"][0].rearrange("(r two) c -> r (two c)", two=2)]
            rows += [w[n][0].rearrange("(r c) -> r c", c=P) for n in ("gn_g", "gn_b")]
            rows += [w["b_gate"][0].rearrange("b (r c) -> (b r) c", c=P), w["pool_scale"][0].rearrange("(r c) -> r c", c=P)]
            at = 0
            for r in rows:
                done = 0
                while done < r.shape[0]:
                    n = min(r.shape[0] - done, P - at % P)
                    pool.dma_start(raw[at % P:at % P + n, at // P, :], r[done:done + n, :]).then_inc(s_raw, 16)
                    done, at = done + n, at + n
            k.n_raw = at
            for i, (c0, n) in enumerate(k.lora_tiles):
                pool.dma_start(k.mu_lora[0:n, i:i + 1], w["mu_shift"][0, c0:c0 + n].rearrange("(n a) -> n a", a=1)).then_inc(s_raw, 16)

        n_dma = 10 + len(k.lora_tiles)

        @block.vector
        def _(dve):
            def rest_of_tile(i):
                _, n, t0 = (tiles[1:] + tiles[:1])[i]
                for q in range(4):
                    g = 4 * i + q + 1
                    dve.wait_ge(s_out, g)
                    rest_bits(nc.vector, k.hT[:, 4 * q:4 * q + 4, t0:t0 + n], tp[q][:, 0:4 * n].rearrange("p (k t) -> p k t", k=4),
                              k.hT_high[:, 4 * q:4 * q + 4, t0:t0 + n]).then_inc(s_rest, 1)

            for i, (x, n, _) in enumerate(tiles[1:] + tiles[:1]):
                if i < 2:
                    dve.wait_ge((s_x0, s_x)[i], (16, 32)[i])
                for j in range(4):
                    nc.vector.bn_stats(stats[0:n, i, j, :], x[:, 512 * j:512 * (j + 1)])
                nc.vector.drain()
                nc.vector.bn_aggr(mv[0:n, i, :], stats[0:n, i, :, :])
                nc.vector.drain()
                nc.vector.tensor_scalar(rs[0:n, i, 0:1], mv[0:n, i, 1:2], LN_EPS, None, ALU.add)
                nc.vector.drain()
                nc.vector.reciprocal(rs[0:n, i, 0:1], rs[0:n, i, 0:1]).then_inc(s_var, 1)
            dve.wait_ge(s_gb, 32)
            for i, (x, n, _) in enumerate(tiles[1:] + tiles[:1]):
                if i:
                    rest_of_tile(i - 1)
                dve.wait_ge(s_rstd, i + 1)
                nc.vector.tensor_scalar(x, x, mv[0:n, i, 0:1], rs[0:n, i, 1:2], ALU.subtract, ALU.mult)
                nc.vector.drain()
                nc.vector.tensor_tensor(x, x, gam[0:n, :], ALU.mult)
                nc.vector.drain()
                nc.vector.tensor_tensor(x, x, bet[0:n, :], ALU.add).then_inc(s_h, 1)
            rest_of_tile(2)
            dve.wait_ge(s_pv, 1)
            nc.vector.tensor_copy(k.vec[:, 0:8, :], pv[:, 0:P].rearrange("p (v r) -> p v r", r=16))
            nc.vector.tensor_copy(k.vec[:, 8:NRAW, :], pv[:, P:P + 64].rearrange("p (v r) -> p v r", r=16))
            nc.vector.tensor_copy(k.pool_scale[:], pv[:, P + 64:P + 72])
            nc.vector.drain()
            nc.vector.tensor_scalar(k.vec[:, V_OMR:V_OMV + 1, :], k.vec[:, V_MUR:V_MUV + 1, :], -1.0, 1.0, ALU.mult, ALU.add)
            nc.vector.tensor_scalar(k.vec[:, V_W0H:V_A0H + 1, :], k.vec[:, V_W0:V_A0 + 1, :], 0.5, None, ALU.mult)
            nc.vector.tensor_scalar(k.om_lora[:], k.mu_lora[:], -1.0, 1.0, ALU.mult, ALU.add)

        @block.scalar
        def _(act):
            for i, (_, n, _) in enumerate(tiles[1:] + tiles[:1]):
                act.wait_ge(s_var, i + 1)
                nc.scalar.activation(rs[0:n, i, 1:2], rs[0:n, i, 0:1], ACT.Sqrt).then_inc(s_rstd, 1)
            g = 0
            for i, (_, n, t0) in enumerate(tiles[1:] + tiles[:1]):
                for q in range(4):
                    g += 1
                    act.wait_ge(s_turn, g)
                    nc.scalar.copy(k.hT_high[:, 4 * q:4 * q + 4, t0:t0 + n].bitcast(F32R),
                                   tp[(g - 1) % 4][:, 0:4 * n].rearrange("p (k t) -> p k t", k=4)).then_inc(s_out, 1)

        @block.tensor
        def _(pe):
            pe.wait_ge(s_const, 16)
            pe.wait_ge(s_raw, 16 * n_dma)
            nc.tensor.transpose(pv[:, 0:P], raw[:, 0, :], ident)
            nc.tensor.transpose(pv[:, P:2 * P], raw[:, 1, :], ident).then_inc(s_pv, 1)
            g = 0
            for i, (x, n, _) in enumerate(tiles[1:] + tiles[:1]):
                pe.wait_ge(s_h, i + 1)
                for q in range(4):
                    g += 1
                    if g > 4:
                        pe.wait_ge(s_rest, g - 4)
                    for j in range(4):
                        mm = nc.tensor.transpose(tp[(g - 1) % 4][:, j * n:(j + 1) * n],
                                                 x[:, (4 * q + j) * P:(4 * q + j + 1) * P], ident[0:n, 0:n])
                    mm.then_inc(s_turn, 1)


def lora_stage(k, w):
    nc = k.nc
    with ExitStack() as ctx:
        raw = k.lora_raw
        wh, wt = (k.sb(f"lora_weights{n}", [P, KT, POOL0 - LORA0], ctx=ctx) for n in ("_high", "_rest"))
        pp = [k.ps(f"lora_project{i}", [P, T], ctx) for i in range(len(k.lora_tiles))]
        s_w, s_split = k.s_lora_w, k.sem("lora_split")
        s_mm, s_own, s_mix = k.sem("lora_projected"), k.sem("lora_own"), k.sem("lora_mixed")
        block = ctx.enter_context(nc.Block())

        @block.tensor
        def _(pe):
            for g in range(4):
                pe.wait_ge(s_split, g + 1)
                for i, (c0, n) in enumerate(k.lora_tiles):
                    for kt in range(4 * g, 4 * g + 4):
                        mm = product(nc, pp[i][0:n, :], [x[:, kt, c0 - LORA0:c0 - LORA0 + n] for x in (wh, wt)],
                                     (k.hT_high[:, kt, :], k.hT[:, kt, :]), kt == 0, kt == KT - 1)
                    if g == 3:
                        mm.then_inc(s_mm, 1)

        @block.vector
        def _(dve):
            for g in range(4):
                dve.wait_ge(s_w[g], 16)
                split(nc, *(x[:, 4 * g:4 * g + 4, :] for x in (wh, wt, raw))).then_inc(s_split, 1)
            for i, (_, n) in enumerate(k.lora_tiles):
                dve.wait_ge(s_own, i + 1)
                nc.vector.scalar_tensor_tensor(out=k.lora[0:n, i, 1:T], in0=pp[i][0:n, 0:T - 1], scalar=k.mu_lora[0:n, i:i + 1],
                                               in1=k.lora[0:n, i, 1:T], op0=ALU.mult, op1=ALU.add).then_inc(s_mix, 1)

        @block.scalar
        def _(act):
            for i, (_, n) in enumerate(k.lora_tiles):
                act.wait_ge(s_mm, i + 1)
                nc.scalar.activation(k.lora[0:n, i, :], pp[i][0:n, :], ACT.Copy, scale=k.om_lora[0:n, i:i + 1]).then_inc(s_own, 1)
            for i, f in ((0, ACT.Tanh), (2, ACT.Sigmoid), (3, ACT.Sigmoid)):
                act.wait_ge(s_mix, i + 1)
                n = k.lora_tiles[i][1]
                nc.scalar.activation(k.lora[0:n, i, :], k.lora[0:n, i, :], f)


ORDER = (
    ("sp", 0), ("sp", 1), ("gr", 0), ("cp", 0), ("r", 0), ("cv", 0), ("rb", 0), ("f", 3), ("u", 0), ("rk", 0),
    ("f", 4), ("Z", 1), ("f", 1), ("t", 0), ("s", 0), ("W", 1), ("r", 1), ("t", 1), ("sp", 2), ("f", 1), ("Z", 2),
    ("t", 2), ("W", 2), ("u", 1), ("s", 1), ("f", 2), ("kn", 0), ("t", 3), ("f", 1), ("Z", 3), ("f", 4), ("r", 2),
    ("sp", 3), ("u", 2), ("lw", 0), ("W", 3), ("f", 1), ("e", 0), ("s", 2), ("Z", 4), ("f", 2), ("la", 0), ("r", 3),
    ("f", 2), ("lg", 0), ("f", 2), ("W", 4), ("u", 3), ("f", 2), ("s", 3), ("sp", 4), ("f", 2), ("r", 4), ("ex", 0),
    ("u", 4), ("Z", 5), ("f", 1), ("nm", 0), ("f", 4), ("s", 4), ("sp", 5), ("W", 5), ("bo", 0), ("yc", 0), ("e", 1),
    ("f", 3), ("gm", 0), ("f", 2), ("ab", 0), ("f", 4), ("gv", 0), ("f", 3), ("ge", 0), ("f", 4), ("e", 2),
)
STAGE = {"sp": 0, "cv": 0, "f": 0, "e": 0, "kn": 1, "lw": 1, "la": 1, "lg": 1, "ex": 1, "nm": 1, "bo": 1, "ab": 1,
         "cp": 2, "gr": 2, "rb": 2, "rk": 2, "Z": 2, "W": 2, "t": 2,
         "r": 3, "u": 3, "s": 3, "yc": 3, "gm": 3, "gv": 3, "ge": 3}


def rwkv_stage(k, w):
    nc = k.nc
    with ExitStack() as ctx:
        sb = lambda name, shape: k.sb(name, shape, ctx=ctx)
        two = lambda name, shape: [sb(f"{name}{i}", shape) for i in range(2)]
        HK = KT // 2
        raw, wh, wt = ([sb(f"w_in{n}{i}", [P, HK, P]) for i in range(2)] for n in ("", "_high", "_rest"))
        ww2, wa2, wg2 = sb("w_decay2", [DECAY_LORA, P]), sb("w_rate2", [ICL_LORA, P]), sb("w_gate2", [P, 2, P])
        cur, gcur = two("pair_vectors", [P, NVEC]), sb("pair_norm_vectors", [P, 2])
        r, kx, v, tmp = two("r", [P, TP]), two("k", [P, TP]), two("v", [P, TP]), sb("shift_part", [P, T])
        sg, am, cs, csm = sb("decay_sigmoid", [P, TP]), sb("rate", [P, TP]), sb("decay_sum", [P, TP]), sb("decay_sum_prev", [P, TP])
        pe_, pi, pm = sb("decay_prod", [P, TP]), sb("decay_prod_inv", [P, TP]), sb("decay_prod_prev", [P, TP])
        kn, sq, rn = sb("k_for_norm", [P, TP]), sb("k_square", [P, TP]), sb("k_rnorm", [P, TP])
        k2, t1, rk = sb("k_mixed", [P, TP]), sb("k_scale", [P, TP]), sb("r_k_prod", [P, TP])
        gate, bon = sb("gate", [P, SEQ]), sb("bonus", [P, SEQ])
        ast, bst, rst = sb("A_st", [P, NCH, CH]), sb("B_st", [P, NCH, CH]), two("R_st", [P, NCH, CH])
        bA, bB, bK, bV = two("A_bd", [P, NCH, P]), sb("B_bd", [P, NCH, P]), sb("K_bd", [P, NCH, P]), sb("V_bd", [P, NCH, P])
        gate3, bon3, ends = two("gate_kept", [P, SEQ]), two("bonus_kept", [P, SEQ]), two("chunk_decay", [P, NCH])
        lt, xs, ys, zs = (sb(n, [P, NCH, CH]) for n in ("LT_st", "X_st", "Y_st", "Z_st"))
        bMT, bY, bZ = two("MT_bd", [P, NCH, P]), two("YI_bd", [P, NCH, P]), sb("Z_bd", [P, NCH, P])
        lev = [sb(f"LT_level{i}_bd", [P, NCH, P]) for i in range(1, LEVELS)]
        rbt, rkt, tok = two("RBT_st", [P, 4, CH]), two("RKT_st", [P, 4, CH]), two("BKV_by_token", [P, 3 * NCH - 2, P])
        rhs, u, spc, s = sb("rhs", [P, P]), sb("U", [P, P]), sb("S_decayed", [P, P]), two("S", [P, P])
        yc, ysq, rstd = sb("y", [P, SEQ]), sb("y_square", [P, SEQ]), sb("y_rstd", [P, SEQ])
        pr = [k.ps(f"project{i}", [P, 512], ctx) for i in range(2)]
        low = k.ps("low_rank", [P, 512], ctx)
        inv = [k.ps(f"invert{i}", [P, 512], ctx) for i in range(3)]
        ch = [k.ps(f"chain{i}", [P, 512], ctx) for i in range(2)]
        c3 = lambda t, n=CH: t.rearrange("p (c t) -> p c t", t=n)

        names = ("w_in0", "w_in1", "high", "split", "lora_w", "project", "own", "shifted", "rm", "lora_mm", "sig", "csum", "exps",
                 "ksq", "norm", "nread", "nrecip", "nsqrt", "rk", "bonus", "bonr", "st", "bdv", "bda", "endc", "cpy", "gram",
                 "maskT", "lread", "mtr", "gram2", "rbr", "levels", "tok_mm", "tok", "X", "Y", "Z", "Zc", "Zst", "WT", "W",
                 "rhs", "rhsc", "U", "Uc", "Snew", "S", "Yo", "Yc", "mean", "center", "sqr", "var", "vrecip", "vsqrt",
                 "done", "zero", "cleared", "seen", "rst")
        q = {n: k.sem(f"r_{n}") for n in names}
        n_zero = 8

        ones = k.const[:, C_ONES:C_ONES + P]
        ident = k.const[:, C_ID:C_ID + P]
        halves = ((slice(0, HEAD), slice(0, CH)), (slice(HEAD, P), slice(CH, P)))
        real = slice(PAD, TP)
        rhs_ps, u_ps, mean_ps, var_ps = ch[0][:, 0:P], ch[0][:, P:2 * P], ch[0][:, 256:512], ch[0][:, 0:256]
        s_ps, y_ps = ch[1][:, 0:P], ch[1][:, P:P + SEQ]

        def mask(c0, n, h=slice(0, P)):
            return k.const[h, c0:c0 + CH].rearrange("p (c t) -> p c t", c=1).to_broadcast((h.stop - h.start, n, CH))

        def by_token(par, n, c):
            return tok[par][:, n * (NCH - 1) + c, :]

        def chunks(i):
            return range(1 if (1 << i) >= META else 0, NCH)

        def schedule(eng, units):
            def step(b, par, lo, hi):
                for name, i in ORDER:
                    if lo <= STAGE[name] <= hi and name in units:
                        units[name](i, b - STAGE[name], (par + STAGE[name]) % 2)

            for b in range(4):
                step(b, b % 2, 0, b)
            with eng.Fori(2, PAIRS // 2) as m:
                step(m * 2, 0, 0, 3)
                step(m * 2 + 1, 1, 0, 3)
            for b in range(PAIRS, PAIRS + 3):
                step(b, b % 2, b - PAIRS + 1, 3)

        W = w["w_in"][0].rearrange("(k p) c -> p k c", p=P)
        Wg = w["w_g2"][0].rearrange("(j p) c -> p j c", p=P)

        block = ctx.enter_context(nc.Block())

        @block.sync
        def _(sp):
            def load(b, first=False):
                for u in range(6):
                    if u > 1 or not first:
                        wait(sp, q["split"], b * 6 + u - 1)
                    sp.dma_start(raw[u % 2][:], W[:, u % 2 * HK:u % 2 * HK + HK, bass.ds(b * P + u // 2 * D, P)]).then_inc(q[f"w_in{u % 2}"], 16)
                if not first:
                    wait(sp, q["lora_mm"], b * 3)
                for dst, src in ((ww2[:], w["w_w2"][0][:, bass.ds(b * P, P)]), (wa2[:], w["w_a2"][0][:, bass.ds(b * P, P)]),
                                 (wg2[:], Wg[:, :, bass.ds(b * P, P)])):
                    sp.dma_start(dst, src).then_inc(q["lora_w"], 16)

            load(0, True)
            with sp.Fori(1, PAIRS) as b:
                load(b)

        @block.gpsimd
        def _(pool):
            for t in (*r, *kx, *v, sg, am):
                nc.gpsimd.memset(t[:, 0:PAD], 0.0).then_inc(q["zero"], 1)

            def cp(_, p, par):
                wait(pool, q["sig"], p * 3 + 3)
                wait(pool, q["bonr"], p + 1)
                wait(pool, q["done"], p - 1)
                wait(pool, q["levels"], p * 10 + 10)
                pool.sem_inc(q["seen"], 1)
                nc.gpsimd.tensor_copy(gate3[par][:], gate[:]).then_inc(q["cpy"], 1)
                nc.gpsimd.tensor_copy(bon3[par][:], bon[:]).then_inc(q["cpy"], 1)

            def gr(_, p, par):
                wait(pool, q["rst"], p + 1)
                splits = p * 6 + 14
                wait(pool, q["split"], min(splits, 6 * PAIRS) if isinstance(splits, int) else splits)
                wait(pool, q["maskT"], p + 1)
                for i in range(1, LEVELS):
                    for h, c in halves:
                        nc.gpsimd.tensor_tensor(lev[i - 1][h, :, c], lt[h], mask(C_LEV + CH * i, NCH, h), ALU.mult).then_inc(q["levels"], 1)

            def sp_(u, b, par):
                wait(pool, q["high"], b * 6 + u + 1)
                rest_bits(nc.gpsimd, wt[u % 2][:], raw[u % 2][:], wh[u % 2][:]).then_inc(q["split"], 1)
                if isinstance(b, int) and b == 0 and u == 1:
                    for t in lev:
                        nc.gpsimd.memset(t[:], 0.0)

            def ab(_, p, par):
                wait(pool, q["shifted"], p * 3 + 3)
                wait(pool, q["Yo"], (p - 1) * 4)
                wait(pool, q["exps"], p + 1)
                nc.gpsimd.tensor_tensor(rst[par][:], c3(r[par][:]), c3(pe_[:]), ALU.mult).then_inc(q["rst"], 1)

            schedule(pool, {"sp": sp_, "cp": cp, "gr": gr, "ab": ab})

        @block.tensor
        def _(pe):
            at = [0]

            def f(n, b, par):
                for _ in range(n):
                    i, kt = divmod(at[0], KT)
                    u, kh = divmod(at[0], HK)
                    if kt == 0:
                        wait(pe, q["own"], b * 3 + i - 1)
                    if kh == 0:
                        wait(pe, q["split"], b * 6 + u + 1)
                    mm = product(nc, pr[(3 * par + i) % 2][:, 0:T], (wh[u % 2][:, kh, :], wt[u % 2][:, kh, :]),
                                 (k.hT_high[:, kt, :], k.hT[:, kt, :]), kt == 0, kt == KT - 1)
                    if kh == HK - 1:
                        mm.then_inc(q["project"], 1)
                    at[0] = (at[0] + 1) % (3 * KT)

            def lw(_, p, par):
                wait(pe, q["lora_w"], p * 48 + 48)
                wait(pe, q["tok"], p * 4)
                wait(pe, q["bonr"], p)
                nc.tensor.matmul(low[:, 0:T], ww2[:], k.lora[0:DECAY_LORA, 0, :], start=True, stop=True).then_inc(q["lora_mm"], 1)

            def la(_, p, par):
                wait(pe, q["sig"], p * 3 + 1)
                nc.tensor.matmul(low[:, 0:T], wa2[:], k.lora[0:ICL_LORA, 1, :], start=True, stop=True).then_inc(q["lora_mm"], 1)

            def lg(_, p, par):
                wait(pe, q["sig"], p * 3 + 2)
                for j in range(2):
                    mm = nc.tensor.matmul(low[:, 0:SEQ], wg2[:, j, :], k.lora[:, 2 + j, META:T], start=(j == 0), stop=(j == 1))
                mm.then_inc(q["lora_mm"], 1)

            def nm(_, p, par):
                wait(pe, q["sig"], p * 3 + 3)
                wait(pe, q["ksq"], p + 1)
                nc.tensor.matmul(low[:, 0:TP], ones, sq[:], start=True, stop=True).then_inc(q["norm"], 1)

            def bo(_, p, par):
                wait(pe, q["nread"], p + 1)
                wait(pe, q["rk"], p + 1)
                nc.tensor.matmul(low[:, 0:SEQ], ones, rk[:, CH:TP], start=True, stop=True).then_inc(q["bonus"], 1)

            def gr(_, p, par):
                wait(pe, q["st"], p + 1)
                wait(pe, q["bda"], p * 3 + 3)
                wait(pe, q["bdv"], p + 1)
                wait(pe, q["Y"], p * LEVELS)
                for n, lhs, rh in ((0, bB, ast), (1, bA[par], bst), (2, bK, ast)):
                    for c in range(NCH):
                        mm = nc.tensor.matmul(inv[n][:, c * CH:(c + 1) * CH], lhs[:, c, :], rh[:, c, :], start=True, stop=True)
                    mm.then_inc(q["gram"], 1)

            def rb(_, p, par):
                wait(pe, q["rst"], p + 1)
                wait(pe, q["maskT"], p + 1)
                for c in range(1, NCH):
                    mm = nc.tensor.matmul(inv[0][:, (c - 1) * CH:c * CH], bB[:, c, :], rst[par][:, c, :], start=True, stop=True)
                mm.then_inc(q["gram2"], 1)

            def rk_(_, p, par):
                wait(pe, q["lread"], p + 1)
                for c in range(1, NCH):
                    mm = nc.tensor.matmul(inv[1][:, (c - 1) * CH:c * CH], bK[:, c, :], rst[par][:, c, :], start=True, stop=True)
                mm.then_inc(q["gram2"], 1)

            order = [(n, c) for n in range(3) for c in range(NCH if n == 2 else NCH - 1)]

            def t(j, p, par):
                if j:
                    wait(pe, q["tok"], p * 4 + j)
                else:
                    wait(pe, q["bonr"], p + 1)
                for m, (n, c) in enumerate(order[4 * j:4 * j + 4]):
                    mm = nc.tensor.transpose(low[:, m * P:(m + 1) * P], (bB, bK, bV)[n][:, c, :], ident)
                mm.then_inc(q["tok_mm"], 1)

            def Z(i, p, par):
                wait(pe, q["levels"], p * 10 + 2 * i)
                wait(pe, q["X"], p * 5 + i)
                if i == 1:
                    wait(pe, q["rbr"], p * 2 + 1)
                else:
                    wait(pe, q["Zst"], p * 4 + i - 1)
                for c in chunks(i):
                    mm = nc.tensor.matmul(inv[0][:, c * CH:(c + 1) * CH], lev[i - 1][:, c, :], xs[:, c, :], start=True, stop=True)
                mm.then_inc(q["Z"], 1)

            def W_(i, p, par):
                wait(pe, q["Zc"], p * 5 + i)
                wait(pe, q["Y"], p * LEVELS + i)
                if i == 1:
                    wait(pe, q["rbr"], p * 2 + 2)
                    wait(pe, q["mtr"], p + 1)
                for c in chunks(i):
                    mm = nc.tensor.matmul(inv[1][:, c * CH:(c + 1) * CH], bZ[:, c, :], ys[:, c, :], start=True, stop=True)
                mm.then_inc(q["WT"], 1)
                if i < LEVELS - 1:
                    wait(pe, q["Zst"], p * 4 + i)
                    for c in chunks(i):
                        mm = nc.tensor.matmul(inv[2][:, c * CH:(c + 1) * CH], bY[par][:, c, :], zs[:, c, :], start=True, stop=True)
                    mm.then_inc(q["W"], 1)

            def r_(c, p, par):
                if c == 0:
                    wait(pe, q["Y"], p * LEVELS + LEVELS)
                    wait(pe, q["tok"], p * 4 + 4)
                    wait(pe, q["vrecip"], p)
                mm = nc.tensor.matmul(rhs_ps, bMT[par][:, c, :], by_token(par, 2, c), start=True, stop=(c == 0))
                if c:
                    wait(pe, q["S"], p * 4 + c)
                    mm = nc.tensor.matmul(rhs_ps, bA[par][:, c, :], s[c % 2][:], start=False, stop=True)
                mm.then_inc(q["rhs"], 1)
                if c > 1:
                    output(c - 1, par)

            def output(c, par):
                y = y_ps[:, (c - 1) * CH:c * CH]
                nc.tensor.matmul(y, s[c % 2][:], rst[par][:, c, :], start=True, stop=False)
                nc.tensor.matmul(y, by_token(par, 2, c), rkt[par][:, c - 1, :], start=False, stop=False)
                nc.tensor.matmul(y, u[:], rbt[par][:, c - 1, :], start=False, stop=True).then_inc(q["Yo"], 1)

            def u_(c, p, par):
                wait(pe, q["rhsc"], p * 5 + c + 1)
                nc.tensor.matmul(u_ps, bY[par][:, c, :], rhs[:], start=True, stop=True).then_inc(q["U"], 1)

            def s_(c, p, par):
                wait(pe, q["Uc"], p * 5 + c + 1)
                if c < NCH - 1:
                    if c == 0:
                        wait(pe, q["Yc"], p)
                    nc.tensor.matmul(s_ps, by_token(par, 1, c), by_token(par, 2, c), start=True, stop=False)
                    nc.tensor.matmul(s_ps, by_token(par, 0, c), u[:], start=False, stop=True).then_inc(q["Snew"], 1)
                else:
                    output(c, par)

            def gm(_, p, par):
                wait(pe, q["Yc"], p + 1)
                nc.tensor.matmul(mean_ps, ones, yc[:], start=True, stop=True).then_inc(q["mean"], 1)

            def gv(_, p, par):
                wait(pe, q["sqr"], p + 1)
                nc.tensor.matmul(var_ps, ones, ysq[:], start=True, stop=True).then_inc(q["var"], 1)

            schedule(pe, {"f": f, "lw": lw, "la": la, "lg": lg, "nm": nm, "bo": bo, "gr": gr, "rb": rb, "rk": rk_, "t": t,
                          "Z": Z, "W": W_, "r": r_, "u": u_, "s": s_, "gm": gm, "gv": gv})

        @block.scalar
        def _(act):
            def e(i, p, par):
                o, m = ((V_OMR, V_MUR), (V_OMK, V_MUK), (V_OMV, V_MUV))[i]
                t = (r, kx, v)[i][par]
                if i == 0:
                    wait(act, q["rm"], p + 1)
                    wait(act, q["st"], p - 1)
                    wait(act, q["rst"], p - 1)
                wait(act, q["project"], p * 6 + 2 * i + 2)
                wait(act, q["shifted"], p * 3 + i)
                nc.scalar.activation(t[:, real], pr[(3 * par + i) % 2][:, 0:T], ACT.Copy, scale=cur[par][:, o:o + 1])
                nc.scalar.activation(tmp[:, 1:T], pr[(3 * par + i) % 2][:, 0:T - 1], ACT.Copy, scale=cur[par][:, m:m + 1]).then_inc(q["own"], 1)

            def lw(_, p, par):
                wait(act, q["csum"], p)
                wait(act, q["lora_mm"], p * 3 + 1)
                nc.scalar.activation(sg[:, real], low[:, 0:T], ACT.Tanh, scale=0.5, bias=cur[par][:, V_W0H:V_W0H + 1]).then_inc(q["sig"], 1)

            def la(_, p, par):
                wait(act, q["st"], p)
                wait(act, q["lora_mm"], p * 3 + 2)
                nc.scalar.activation(am[:, real], low[:, 0:T], ACT.Tanh, scale=0.5, bias=cur[par][:, V_A0H:V_A0H + 1]).then_inc(q["sig"], 1)

            def lg(_, p, par):
                wait(act, q["cpy"], p * 2)
                wait(act, q["lora_mm"], p * 3 + 3)
                nc.scalar.copy(gate[:], low[:, 0:SEQ]).then_inc(q["sig"], 1)

            def ex(_, p, par):
                wait(act, q["endc"], p)
                wait(act, q["rst"], p)
                wait(act, q["csum"], p + 1)
                nc.scalar.activation(pe_[:], cs[:], ACT.Exp, scale=-DECAY)
                nc.scalar.activation(pi[:], cs[:], ACT.Exp, scale=DECAY)
                nc.scalar.activation(pm[:], csm[:], ACT.Exp, scale=-DECAY).then_inc(q["exps"], 1)

            def nm(_, p, par):
                wait(act, q["nrecip"], p + 1)
                nc.scalar.activation(rn[:], rn[:], ACT.Sqrt).then_inc(q["nsqrt"], 1)

            def ab(_, p, par):
                if isinstance(p, int) and p == 0:
                    act.wait_ge(q["cleared"], 1)
                wait(act, q["shifted"], p * 3 + 3)
                wait(act, q["tok"], p * 4)
                for h, c in halves:
                    ins = nc.scalar.copy(bV[h, :, c], c3(v[par][h]))
                ins.then_inc(q["bda"], 1)
                wait(act, q["st"], p + 1)
                wait(act, q["Yo"], (p - 1) * 4)
                for dst, t in ((bA[par], ast), (bB, bst)):
                    for h, c in halves:
                        ins = nc.scalar.copy(dst[h, :, c], t[h])
                    ins.then_inc(q["bda"], 1)

            def t(j, p, par):
                wait(act, q["tok_mm"], p * 4 + j + 1)
                n = min(4, 3 * NCH - 2 - 4 * j) * P
                dst = tok[par][:].rearrange("p a b -> p (a b)")[:, 4 * j * P:4 * j * P + n]
                nc.scalar.copy(dst, low[:, 0:n]).then_inc(q["tok"], 1)

            def Z(i, p, par):
                if i < LEVELS - 1:
                    wait(act, q["W"], p * 4 + i - 1)
                    wait(act, q["Zc"], p * 5 + i)
                    c0 = chunks(i).start
                    nc.scalar.copy(zs[:, c0:], c3(inv[0][:, c0 * CH:TP])).then_inc(q["Zst"], 1)

            def r_(c, p, par):
                wait(act, q["rhs"], p * 5 + c + 1)
                nc.scalar.copy(rhs[:], rhs_ps).then_inc(q["rhsc"], 1)

            def u_(c, p, par):
                wait(act, q["U"], p * 5 + c + 1)
                nc.scalar.copy(u[:], u_ps).then_inc(q["Uc"], 1)

            def y(_, p, par):
                wait(act, q["done"], p)
                wait(act, q["Yo"], p * 4 + 4)
                nc.scalar.copy(yc[:], y_ps).then_inc(q["Yc"], 1)

            def gm(_, p, par):
                wait(act, q["center"], p + 1)
                nc.scalar.activation(ysq[:], yc[:], ACT.Square).then_inc(q["sqr"], 1)

            def ge(_, p, par):
                wait(act, q["vrecip"], p + 1)
                nc.scalar.activation(rstd[:], rstd[:], ACT.Sqrt).then_inc(q["vsqrt"], 1)

            wait(act, q["zero"], n_zero)
            schedule(act, {"e": e, "lw": lw, "la": la, "lg": lg, "ex": ex, "nm": nm, "ab": ab, "t": t, "Z": Z, "r": r_, "u": u_, "yc": y, "gm": gm, "ge": ge})

        @block.vector
        def _(dve):
            d, n = nc.vector.drain, nc.vector

            def sp_(u, b, par):
                wait(dve, q["project"], b * 6 + u - 1)
                wait(dve, q[f"w_in{u % 2}"], b * 48 + 16 * (u // 2) + 16)
                leading_bits(nc, wh[u % 2][:], raw[u % 2][:]).then_inc(q["high"], 1)

            def cv(_, p, par):
                d()
                n.tensor_copy(cur[par][:], k.vec[:, :, bass.ds(p, 1)].rearrange("p v a -> p (v a)")).then_inc(q["rm"], 1)
                if isinstance(p, int) and p == 0:
                    for t in (*bA, bB, bK, bV, *bMT, *bY, bZ):
                        ins = n.memset(t[:], 0.0)
                    ins.then_inc(q["cleared"], 1)

            def e(i, p, par):
                t = (r, kx, v)[i][par][:, PAD + 1:]
                wait(dve, q["own"], p * 3 + i + 1)
                n.tensor_tensor(t, t, tmp[:, 1:T], ALU.add).then_inc(q["shifted"], 1)

            def kn_(_, p, par):
                d()
                n.tensor_scalar(kn[:], kx[par][:], cur[par][:, V_KK:V_KK + 1], None, ALU.mult)
                d()
                n.tensor_tensor(sq[:], kn[:], kn[:], ALU.mult).then_inc(q["ksq"], 1)

            def la(_, p, par):
                wait(dve, q["sig"], p * 3 + 2)
                n.tensor_scalar(sg[:, real], sg[:, real], 0.5, 0.5, ALU.mult, ALU.add)
                n.tensor_scalar(am[:, real], am[:, real], 0.5, -0.5, ALU.mult, ALU.add)
                d()
                n.tensor_tensor_scan(cs[:], k.const[:, C_SCAN:C_SCAN + TP], sg[:], 0.0, ALU.mult, ALU.add)
                n.tensor_scalar(t1[:], am[:], cur[par][:, V_KA:V_KA + 1], 1.0, ALU.mult, ALU.add)
                d()
                n.tensor_tensor(csm[:], cs[:], sg[:], ALU.subtract).then_inc(q["csum"], 1)
                n.tensor_tensor(k2[:], kx[par][:], t1[:], ALU.mult)
                d()
                n.scalar_tensor_tensor(out=rk[:], in0=r[par][:], scalar=cur[par][:, V_RK:V_RK + 1], in1=k2[:],
                                       op0=ALU.mult, op1=ALU.mult).then_inc(q["rk"], 1)

            def nm(_, p, par):
                wait(dve, q["norm"], p + 1)
                n.tensor_scalar(rn[:], low[:, 0:TP], 1e-24, None, ALU.max).then_inc(q["nread"], 1)
                d()
                n.reciprocal(rn[:], rn[:]).then_inc(q["nrecip"], 1)

            def bo(_, p, par):
                wait(dve, q["cpy"], p * 2)
                wait(dve, q["bonus"], p + 1)
                n.tensor_tensor(bon[:], low[:, 0:SEQ], v[par][:, CH:TP], ALU.mult).then_inc(q["bonr"], 1)

            def ab(_, p, par):
                wait(dve, q["exps"], p + 1)
                for h, c in halves:
                    ins = n.tensor_tensor(bK[h, :, c], c3(k2[h]), c3(pi[h]), ALU.mult)
                ins.then_inc(q["bdv"], 1)
                wait(dve, q["nsqrt"], p + 1)
                n.tensor_tensor(kn[:], kn[:], rn[:], ALU.mult)
                d()
                n.tensor_tensor(ast[:], c3(kn[:]), c3(pm[:]), ALU.mult)
                n.scalar_tensor_tensor(out=k2[:], in0=am[:], scalar=1.0, in1=kn[:], op0=ALU.add, op1=ALU.mult)
                d()
                n.scalar_tensor_tensor(out=bst[:], in0=c3(k2[:]), scalar=-1.0, in1=c3(pi[:]), op0=ALU.mult, op1=ALU.mult).then_inc(q["st"], 1)

            def gr(_, p, par):
                n.tensor_copy(ends[par][:], pe_[:, CH - 1::CH]).then_inc(q["endc"], 1)
                wait(dve, q["gram"], p * 3 + 1)
                n.tensor_tensor(lt[:], c3(inv[0][:, 0:TP]), mask(C_SU, NCH), ALU.mult).then_inc(q["maskT"], 1)
                wait(dve, q["gram"], p * 3 + 2)
                n.tensor_tensor(xs[:], c3(inv[1][:, 0:TP]), mask(C_M1, NCH), ALU.mult).then_inc(q["lread"], 1)
                d()
                n.tensor_tensor(xs[:], xs[:], mask(C_IST, NCH), ALU.add).then_inc(q["X"], 1)
                n.tensor_tensor(ys[:], lt[:], mask(C_LEV, NCH), ALU.mult)
                d()
                n.tensor_tensor(ys[:], ys[:], mask(C_IST, NCH), ALU.add)
                d()
                for h, c in halves:
                    ins = n.tensor_copy(bY[par][h, :, c], ys[h])
                ins.then_inc(q["Y"], 1)

            def rb(_, p, par):
                wait(dve, q["gram2"], p * 2 + 1)
                n.tensor_tensor(rbt[par][:], c3(inv[0][:, 0:SEQ]), mask(C_IU, 4), ALU.mult).then_inc(q["rbr"], 1)

            def rk_(_, p, par):
                wait(dve, q["gram2"], p * 2 + 2)
                n.tensor_tensor(rkt[par][:], c3(inv[1][:, 0:SEQ]), mask(C_IU, 4), ALU.mult).then_inc(q["rbr"], 1)
                for h, c in halves:
                    ins = n.tensor_tensor(bMT[par][h, :, c], c3(inv[2][h, 0:TP]), mask(C_SU, NCH, h), ALU.mult)
                ins.then_inc(q["mtr"], 1)

            def Z(i, p, par):
                wait(dve, q["Z"], p * 5 + i)
                c0 = chunks(i).start
                for h, c in halves:
                    ins = n.tensor_copy(bZ[h, c0:, c], c3(inv[0][h, c0 * CH:TP]))
                ins.then_inc(q["Zc"], 1)

            def W_(i, p, par):
                wait(dve, q["WT"], p * 5 + i)
                c0 = chunks(i).start
                add = slice(c0 * CH, TP)
                if i < LEVELS - 1:
                    n.tensor_tensor(ys[:, c0:], ys[:, c0:], c3(inv[1][:, add]), ALU.add)
                    wait(dve, q["W"], p * 4 + i)
                    n.tensor_tensor(xs[:, c0:], xs[:, c0:], c3(inv[2][:, add]), ALU.add).then_inc(q["X"], 1)
                    d()
                    for h, c in halves:
                        ins = n.tensor_copy(bY[par][h, c0:, c], ys[h, c0:])
                else:
                    for h, c in halves:
                        ins = n.tensor_tensor(bY[par][h, c0:, c], ys[h, c0:], c3(inv[1][h, add]), ALU.add)
                ins.then_inc(q["Y"], 1)

            def r_(c, p, par):
                if 0 < c < NCH - 1:
                    n.tensor_scalar(spc[:], s[c % 2][:], ends[par][:, c:c + 1], None, ALU.mult)

            def s_(c, p, par):
                if c < NCH - 1:
                    d()
                    wait(dve, q["Snew"], p * 4 + c + 1)
                    end, new = ends[par][:, c:c + 1], s[(c + 1) % 2][:]
                    if c:
                        ins = n.scalar_tensor_tensor(out=new, in0=s_ps, scalar=end, in1=spc[:], op0=ALU.mult, op1=ALU.add)
                    else:
                        ins = n.tensor_scalar(new, s_ps, end, None, ALU.mult)
                    ins.then_inc(q["S"], 1)
                    d()

            def gm(_, p, par):
                n.tensor_copy(gcur[:], k.vec[:, V_GNG:V_GNB + 1, bass.ds(p, 1)].rearrange("p v a -> p (v a)"))
                wait(dve, q["mean"], p + 1)
                n.scalar_tensor_tensor(out=yc[:], in0=mean_ps, scalar=-1.0 / HEAD, in1=yc[:], op0=ALU.mult, op1=ALU.add).then_inc(q["center"], 1)

            def gv(_, p, par):
                wait(dve, q["var"], p + 1)
                n.tensor_scalar(rstd[:], var_ps, 1.0 / HEAD, GN_EPS, ALU.mult, ALU.add)
                d()
                n.reciprocal(rstd[:], rstd[:]).then_inc(q["vrecip"], 1)

            def ge(_, p, par):
                wait(dve, q["cpy"], p * 2 + 2)
                wait(dve, q["vsqrt"], p + 1)
                n.tensor_tensor(yc[:], yc[:], rstd[:], ALU.mult)
                d()
                n.tensor_scalar(yc[:], yc[:], gcur[:, 0:1], gcur[:, 1:2], ALU.mult, ALU.add)
                d()
                n.tensor_tensor(yc[:], yc[:], bon3[par][:], ALU.add)
                d()
                n.tensor_tensor(k.yaT[:, bass.ds(p, 1), :].rearrange("p a t -> p (a t)"), yc[:], gate3[par][:], ALU.mult).then_inc(q["done"], 1)

            wait(dve, q["zero"], n_zero)
            schedule(dve, {"sp": sp_, "cv": cv, "e": e, "kn": kn_, "la": la, "nm": nm, "bo": bo, "ab": ab, "gr": gr, "rb": rb, "rk": rk_,
                           "Z": Z, "W": W_, "r": r_, "s": s_, "gm": gm, "gv": gv, "ge": ge})


def norm_stats(nc, x, n, stats, mv, rs):
    for j in range(4):
        nc.vector.bn_stats(stats[0:n, j, :], x[:, 512 * j:512 * (j + 1)])
    return norm_variance(nc, n, stats, mv, rs)


def norm_variance(nc, n, stats, mv, rs):
    nc.vector.drain()
    nc.vector.bn_aggr(mv[0:n, :], stats[0:n, :, :])
    nc.vector.drain()
    nc.vector.tensor_scalar(rs[0:n, 0:1], mv[0:n, 1:2], LN_EPS, None, ALU.add)
    nc.vector.drain()
    return nc.vector.reciprocal(rs[0:n, 1:2], rs[0:n, 0:1])


def norm_apply(nc, x, n, mv, rs, gamma, beta):
    y, t = rs[0:n, 2:3], rs[0:n, 3:4]
    nc.vector.drain()
    nc.vector.tensor_scalar(t, y, y, rs[0:n, 0:1], ALU.mult, ALU.mult)
    nc.vector.drain()
    nc.vector.tensor_scalar(t, t, -0.5, 1.5, ALU.mult, ALU.add)
    nc.vector.drain()
    nc.vector.tensor_tensor(y, y, t, ALU.mult)
    nc.vector.drain()
    nc.vector.tensor_scalar(x, x, mv[0:n, 0:1], y, ALU.subtract, ALU.mult)
    nc.vector.drain()
    nc.vector.tensor_tensor(x, x, gamma[0:n, :], ALU.mult)
    nc.vector.drain()
    return nc.vector.tensor_tensor(x, x, beta[0:n, :], ALU.add)


def row_broadcast(v):
    return v.rearrange("(a d) -> a d", a=1).to_broadcast((P, D))


def pool_stage(k, w):
    nc = k.nc
    groups, gd = len(POOL_WINDOWS), POOL_DIM // len(POOL_WINDOWS)
    gt = gd // P
    with ExitStack() as ctx:
        HK = KT // 2
        raw = k.sb("pool_weights", [P, KT, gd], ctx=ctx)
        wh, wt = ([k.sb(f"pool_weights{n}{i}", [P, KT, gd], ctx=ctx) for i in range(2)] for n in ("_high", "_rest"))
        wm = k.sb("pool_mix", [P, groups, gt, gd], ctx=ctx)
        uu = k.sb("pool_in", [P, 2, gt, T], ctx=ctx)
        sm = k.sb("pool_sums", [P, 2, gt, T], ctx=ctx)
        pd = k.sb("pooled", [P, 2, gt, SEQ], ctx=ctx)
        pu = [[k.ps(f"pool_u{i}{j}", [P, 512], ctx) for j in range(gt)] for i in range(2)]
        pm = [[k.ps(f"pool_m{i}{j}", [P, 512], ctx) for j in range(gt)] for i in range(2)]
        s_w, s_wm = [k.sem("pool_w0"), k.sem("pool_w1")], k.sem("pool_wm")
        s_split, s_rest = k.sem("pool_split"), k.sem("pool_rest")
        s_u, s_uc, s_pd, s_m, s_y = k.sem("pool_u"), k.sem("pool_uc"), k.sem("pool_d"), k.sem("pool_m"), k.sem("pool_y")
        src = w["w_in"][0].rearrange("(k p) c -> p k c", p=P)
        block = ctx.enter_context(nc.Block())

        @block.sync
        def _(sp):
            for g in range(groups):
                for h in range(2):
                    wait(sp, s_split, 2 * (g - 1) + h + 1)
                    sp.dma_start(raw[:, h * HK:(h + 1) * HK], src[:, h * HK:(h + 1) * HK, POOL0 + g * gd:POOL0 + (g + 1) * gd]).then_inc(s_w[h], 16)
                if g == 0:
                    for h in range(groups):
                        sp.dma_start(wm[:, h, :, :], w["w_pool"][0, h].rearrange("(j p) d -> p j d", p=P)).then_inc(s_wm, 16)

        @block.tensor
        def _(pe):
            def mix(g):
                wait(pe, s_pd, g + 1)
                wait(pe, s_rest, gt * (g - 1))
                for j in range(gt):
                    for i in range(gt):
                        mm = nc.tensor.matmul(pm[g % 2][j][:, 0:SEQ], wm[:, g, i, j * P:(j + 1) * P], pd[:, g % 2, i, :],
                                              start=(i == 0), stop=(i == gt - 1))
                    mm.then_inc(s_m, 1)

            for g in range(groups):
                wait(pe, s_uc, gt * (g - 1))
                for j in range(gt):
                    for kt in range(KT):
                        if j == 0 and kt % HK == 0:
                            wait(pe, s_split, 2 * g + kt // HK + 1)
                        mm = product(nc, pu[g % 2][j][:, 0:T], [x[g % 2][:, kt, j * P:(j + 1) * P] for x in (wh, wt)],
                                     (k.hT_high[:, kt, :], k.hT[:, kt, :]), kt == 0, kt == KT - 1)
                    mm.then_inc(s_u, 1)
                if g == 1:
                    pe.wait_ge(s_wm, 16 * groups)
                if g:
                    mix(g - 1)
            mix(groups - 1)

        @block.vector
        def _(dve):
            def parts(g):
                wait(dve, s_u, gt * (g - 1))
                for h in range(2):
                    dve.wait_ge(s_w[h], 16 * g + 16)
                    split(nc, *(x[:, h * HK:(h + 1) * HK] for x in (wh[g % 2], wt[g % 2], raw))).then_inc(s_split, 1)

            def rest(g):
                for j in range(gt):
                    m = g * gt + j
                    dve.wait_ge(s_y, m + 1)
                    nc.vector.scalar_tensor_tensor(out=k.ybT[:, m, :].bitcast(F32R), in0=pm[g % 2][j][:, 0:SEQ], scalar=k.pool_scale[:, m:m + 1],
                                                   in1=k.ybT_high[:, m, :], op0=ALU.mult, op1=ALU.subtract).then_inc(s_rest, 1)

            parts(0)
            for g, window in enumerate(POOL_WINDOWS):
                if g < groups - 1:
                    parts(g + 1)
                a, b = uu[:, g % 2], sm[:, g % 2]
                dve.wait_ge(s_uc, gt * (g + 1))
                src_, dst, size, c0 = a, b, 1, 0
                nc.vector.tensor_tensor(b[:, :, 1:], a[:, :, 1:], a[:, :, 0:T - 1], ALU.add)
                size, c0 = 2, 1
                while size < window:
                    nc.vector.drain()
                    nc.vector.tensor_tensor(k.pool_tmp[:, :, c0 + size:], b[:, :, c0 + size:], b[:, :, c0:T - size], ALU.add)
                    c0, size = c0 + size, 2 * size
                    nc.vector.drain()
                    nc.vector.tensor_copy(b[:, :, c0:], k.pool_tmp[:, :, c0:])
                nc.vector.drain()
                wait(dve, s_m, gt * (g - 1))
                nc.vector.scalar_tensor_tensor(out=pd[:, g % 2], in0=b[:, :, META:], scalar=1.0 / window, in1=a[:, :, META:],
                                               op0=ALU.mult, op1=ALU.subtract).then_inc(s_pd, 1)
                if g:
                    rest(g - 1)
            rest(groups - 1)

        @block.scalar
        def _(act):
            def out(g):
                for j in range(gt):
                    act.wait_ge(s_m, gt * g + j + 1)
                    m = g * gt + j
                    nc.scalar.activation(k.ybT_high[:, m, :].bitcast(F32R), pm[g % 2][j][:, 0:SEQ], ACT.Copy,
                                         scale=k.pool_scale[:, m:m + 1]).then_inc(s_y, 1)

            for g in range(groups):
                wait(act, s_pd, g - 1)
                for j in range(gt):
                    act.wait_ge(s_u, gt * g + j + 1)
                    nc.scalar.copy(uu[:, g % 2, j, :], pu[g % 2][j][:, 0:T]).then_inc(s_uc, 1)
                if g:
                    out(g - 1)
            out(groups - 1)


def merge_stage(k, w):
    nc = k.nc
    with ExitStack() as ctx:
        HK = KT // 2
        halves = [(n, h) for n, kts in enumerate((KT, KT, KT, KT // 2)) for h in range(kts // HK)]
        raw, wh, wt = ([k.sb(f"merge_w{n}{i}", [P, HK, P], ctx=ctx) for i in range(2)] for n in ("", "_high", "_rest"))
        ya_high, ya_rest = k.sb("yaT_high", [P, KT, SEQ], ctx=ctx), k.sb("yaT_rest", [P, KT, SEQ], ctx=ctx)
        gt = [k.sb(f"merge_gates{i}", [P, 2, SEQ], ctx=ctx) for i in range(2)]
        bias = k.sb("merge_bias", [P, 4], ctx=ctx)
        ps = [[k.ps(f"merge_ps{i}{n}", [P, 512], ctx) for n in range(4)] for i in range(2)]
        s_w, s_split, s_y = [k.sem(f"merge_w{i}") for i in range(2)], k.sem("merge_split"), k.sem("merge_y_split")
        s_half = k.sem("merge_half")
        s_gate = [k.sem(f"merge_gate{i}") for i in range(2)]
        s_load = k.sem("merge_load")
        s_bias, s_done = k.sem("merge_bias"), [k.sem(f"merge_done{i}") for i in range(2)]
        W = w["w_in"][0].rearrange("(k p) c -> p k c", p=P)
        A = w["w_branch_a"][0].rearrange("(k p) c -> p k c", p=P)
        B = w["w_branch_b"][0].rearrange("(k p) c -> p k c", p=P)
        STEPS = KT // 2
        block = ctx.enter_context(nc.Block())

        @block.sync
        def _(sp):
            def load(m, first=False):
                col = 0 if first else sp.snap(m * (2 * P))
                for i in range(2):
                    for u, (n, h) in enumerate(halves):
                        at = 7 * i + u
                        if at > 1 or not first:
                            wait(sp, s_split, m * 14 + at - 1)
                            if not first:
                                sp.sem_inc(s_load, 1)
                        src, c0 = ((W, GATE0), (W, GATE0 + D), (A, 0), (B, 0))[n]
                        sp.dma_start(raw[at % 2][:], src[:, h * HK:(h + 1) * HK, bass.ds(col + (c0 + i * P), P)]).then_inc(s_w[at % 2], 16)

            load(0, True)
            for i in range(2):
                sp.dma_start(k.out_raw[i][:], w["w_out"][0].rearrange("(k p) c -> p k c", p=P)[:, 4 * i:4 * i + 4, 0:512]).then_inc(k.s_out_w[i], 16)
            with sp.Fori(1, STEPS) as m:
                load(m)

        @block.tensor
        def _(pe):
            def step(m, first=False):
                for i in range(2):
                    if not first:
                        wait(pe, s_done[i], m)
                    for u, (n, h) in enumerate(halves):
                        xs = ((k.hT_high[:, :, META:T], k.hT[:, :, META:T]),) * 2 + ((ya_high, ya_rest), (k.ybT_high, k.ybT))
                        if first and i == 0 and n == 2:
                            pe.wait_ge(s_y, 1)
                        wait(pe, s_split, m * 14 + 7 * i + u + 1)
                        last = u + 1 == len(halves) or halves[u + 1][0] != n
                        for kh in range(HK):
                            kt = h * HK + kh
                            mm = product(nc, ps[i][n][:, 0:SEQ], [x[(7 * i + u) % 2][:, kh, :] for x in (wh, wt)],
                                         [x[:, kt, :] for x in xs[n]], kt == 0, last and kh == HK - 1)
                        mm.then_inc(s_half, 1)

            step(0, True)
            with pe.Fori(1, STEPS) as m:
                step(m)

        @block.scalar
        def _(act):
            def step(m, first=False):
                wait(act, s_bias, m + 1)
                for i in range(2):
                    for n in range(2):
                        wait(act, s_half, m * 14 + 7 * i + 2 * n + 2)
                        nc.scalar.activation(gt[i][:, n, :], ps[i][n][:, 0:SEQ], ACT.Sigmoid, bias=bias[:, 2 * n + i:2 * n + i + 1]).then_inc(s_gate[i], 1)

            step(0, True)
            with act.Fori(1, STEPS) as m:
                step(m)

        @block.vector
        def _(dve):
            def parts(m, i, us, first=False):
                for u in us:
                    at = 7 * i + u
                    if at > 1 or not first:
                        wait(dve, s_half, m * 14 + at - 1)
                    wait(dve, s_w[at % 2], m * 112 + 16 * (at // 2) + 16)
                    split(nc, wh[at % 2][:], wt[at % 2][:], raw[at % 2][:]).then_inc(s_split, 1)

            def finish(m, i):
                wait(dve, s_gate[i], m * 2 + 2)
                g = gt[i]
                for n in range(2):
                    wait(dve, s_half, m * 14 + 7 * i + 6 + n)
                    nc.vector.tensor_tensor(g[:, n, :], g[:, n, :], ps[i][2 + n][:, 0:SEQ], ALU.mult)
                nc.vector.drain()
                nc.vector.tensor_tensor(g[:, 0, :], g[:, 0, :], g[:, 1, :], ALU.add)

            def keep(m, i):
                g = gt[i]
                nc.vector.drain()
                leading_bits(nc, g[:, 1, :], g[:, 0, :])
                nc.vector.drain()
                at = bass.ds(m * 2 + i, 1)
                leading_bits(nc, k.mT_high[:, at, :].rearrange("p a t -> p (a t)"), g[:, 1, :])
                rest_bits(nc.vector, k.mT[:, at, :].rearrange("p a t -> p (a t)"), g[:, 0, :], g[:, 1, :]).then_inc(s_done[i], 1)

            def step(m, last=False):
                nc.vector.tensor_copy(bias[:].rearrange("p (v a) -> p v a", v=2), k.vec[:, V_BG0:V_BG1 + 1, bass.ds(m * 2, 2)]).then_inc(s_bias, 1)
                parts(m, 1, range(2))
                finish(m, 0)
                parts(m, 1, range(2, 3))
                keep(m, 0)
                parts(m, 1, range(3, 7))
                if not last:
                    parts(m + 1, 0, range(2))
                finish(m, 1)
                if not last:
                    parts(m + 1, 0, range(2, 3))
                keep(m, 1)
                if not last:
                    parts(m + 1, 0, range(3, 7))

            parts(0, 0, range(2), True)
            split(nc, ya_high[:], ya_rest[:], k.yaT[:]).then_inc(s_y, 1)
            parts(0, 0, range(2, 7), True)
            step(0)
            with dve.Fori(1, STEPS - 1) as m:
                step(m)
            step(STEPS - 1, True)


def out_stage(k, w):
    nc = k.nc
    NB = D // 512
    with ExitStack() as ctx:
        QK = KT // 4
        raw = k.out_raw
        wh, wt = ([k.sb(f"out_w{n}{i}", [P, QK, 512], ctx=ctx) for i in range(2)] for n in ("_high", "_rest"))
        gam, bet = (k.sb(f"ln1_{n}", [P, D], ctx=ctx)[:, :] for n in ("gamma", "beta"))
        stats, mv, rs = k.sb("ln1_stats", [P, TT, 4, 6], ctx=ctx), k.sb("ln1_mv", [P, TT, 2], ctx=ctx), k.sb("ln1_rs", [P, TT, 4], ctx=ctx)
        ps = [[k.ps(f"out_ps{i}{t}", [P, 512], ctx) for t in range(TT)] for i in range(2)]
        tp = [k.ps(f"out_turn{i}", [P, 512], ctx) for i in range(4)]
        s_w, s_gb = k.s_out_w, k.sem("out_gb")
        s_split, s_quarter = k.sem("out_split"), k.sem("out_quarter")
        s_mm = [k.sem("out_mm0"), k.sem("out_mm1")]
        s_ev = [k.sem("out_ev0"), k.sem("out_ev1")]
        s_var, s_rt, s_h, s_tp, s_tc = k.sem("ln1_var"), k.sem("ln1_root"), k.sem("ln1_h"), k.sem("ln1_turn"), k.sem("ln1_turned")
        W = w["w_out"][0].rearrange("(k p) c -> p k c", p=P)
        ident = k.const[:, C_ID:C_ID + P]
        block = ctx.enter_context(nc.Block())

        @block.sync
        def _(sp):
            for n in range(NB):
                for q4 in range(4):
                    if n == 0 and q4 < 2:
                        continue
                    wait(sp, s_split, 4 * n + q4 - 1)
                    sp.dma_start(raw[q4 % 2][:], W[:, q4 * QK:(q4 + 1) * QK, n * 512:(n + 1) * 512]).then_inc(s_w[q4 % 2], 16)
            sp.dma_start(gam, row_broadcast(w["ln1_g"][0])).then_inc(s_gb, 16)
            sp.dma_start(bet, row_broadcast(w["ln1_b"][0])).then_inc(s_gb, 16)
            for i in range(2):
                sp.wait_ge(s_split, 4 * NB - 1 + i)
                sp.dma_start(k.query_raw[i], w["w_q_peer"][0].rearrange("(k p) c -> p k c", p=P)[:, :, i * P:(i + 1) * P]).then_inc(k.s_query_w[i], 16)

        @block.tensor
        def _(pe):
            def step(m, first=False):
                for i in range(2):
                    if not first:
                        wait(pe, s_ev[i], m * TT)
                    for q4 in range(4):
                        wait(pe, s_split, m * 8 + 4 * i + q4 + 1)
                        for t in range(TT):
                            for kh in range(QK):
                                kt = q4 * QK + kh
                                mm = product(nc, ps[i][t][:], [x[:, kt, t * P:(t + 1) * P] for x in (k.mT_high, k.mT)],
                                             (wh[q4 % 2][:, kh, :], wt[q4 % 2][:, kh, :]), kt == 0, kt == KT - 1)
                            if q4 == 3:
                                mm.then_inc(s_mm[i], 1)
                        if q4 < 3:
                            mm.then_inc(s_quarter, 1)

            step(0, True)
            with pe.Fori(1, NB // 2) as m:
                step(m)
            for t in range(TT):
                pe.wait_ge(s_h, t + 1)
                for q4 in range(4):
                    n = t * 4 + q4
                    wait(pe, s_tc, n - 3)
                    for j in range(4):
                        mm = nc.tensor.transpose(tp[q4][:, j * P:(j + 1) * P], k.h[:, t, (4 * q4 + j) * P:(4 * q4 + j + 1) * P], ident)
                    mm.then_inc(s_tp, 1)

        @block.vector
        def _(dve):
            def parts(n, quarters):
                for q4 in quarters:
                    if q4 > 1:
                        dve.wait_ge(s_quarter, 3 * n + q4 - 1)
                    elif n:
                        (dve.wait_ge(s_mm[(n - 1) % 2], TT * ((n - 1) // 2 + 1)) if q4 else dve.wait_ge(s_quarter, 3 * n))
                    dve.wait_ge(s_w[q4 % 2], 32 * n + 16 * (q4 // 2) + 16)
                    split(nc, wh[q4 % 2][:], wt[q4 % 2][:], raw[q4 % 2][:]).then_inc(s_split, 1)

            parts(0, range(4))
            for n in range(NB):
                if n < NB - 1:
                    parts(n + 1, range(2))
                for t in range(TT):
                    dve.wait_ge(s_mm[n % 2], n // 2 * TT + t + 1)
                    x = k.h[:, t, n * 512:(n + 1) * 512]
                    nc.vector.scalar_tensor_tensor(out=x, in0=x, scalar=ALPHA, in1=ps[n % 2][t][:], op0=ALU.mult, op1=ALU.add).then_inc(s_ev[n % 2], 1)
                nc.vector.drain()
                for t in range(TT):
                    nc.vector.bn_stats(stats[:, t, n, :], k.h[:, t, n * 512:(n + 1) * 512])
                if n < NB - 1:
                    parts(n + 1, range(2, 4))
            for t in range(TT):
                norm_variance(nc, P, stats[:, t], mv[:, t], rs[:, t]).then_inc(s_var, 1)
            dve.wait_ge(s_gb, 32)
            for t in range(TT):
                dve.wait_ge(s_rt, t + 1)
                norm_apply(nc, k.h[:, t, :], P, mv[:, t], rs[:, t], gam, bet).then_inc(s_h, 1)

        @block.scalar
        def _(act):
            for t in range(TT):
                act.wait_ge(s_var, t + 1)
                nc.scalar.activation(rs[:, t, 2:3], rs[:, t, 1:2], ACT.Sqrt).then_inc(s_rt, 1)
            for t in range(TT):
                for q4 in range(4):
                    act.wait_ge(s_tp, t * 4 + q4 + 1)
                    nc.scalar.copy(k.h1T[:, 4 * q4:4 * q4 + 4, t * P:(t + 1) * P], tp[q4][:].rearrange("p (j t) -> p j t", t=P)).then_inc(s_tc, 1)


def router_stage(k, w):
    nc = k.nc
    NEG = -3.0e38
    with ExitStack() as ctx:
        sb = lambda name, shape, dt=F32: k.sb(name, shape, dt, ctx=ctx)
        wt = [k.query_raw, [sb(f"query_w1{i}", [P, KT, P]) for i in range(2)]]
        keys, kT = sb("keys", [P, 2, P]), sb("keysT", [P, 2, P])
        qT = [sb(f"queryT{i}", [P, SEQ]) for i in range(2)]
        sc, sc2 = sb("scores", [P, TT, 2, N_KEYS]), sb("scores_left", [P, TT, 2, N_KEYS])
        sv, si = sb("side_best", [P, TT, 2, TOPK]), sb("side_index", [P, TT, 2, TOPK], U32)
        sif = sb("side_index_f", [P, TT, 2, TOPK])
        cand, cand2 = sb("candidates", [P, TT, TOPK, TOPK]), sb("candidates_left", [P, TT, TOPK * TOPK])
        tv, ti = sb("top", [P, TT, TOPK]), sb("top_pos", [P, TT, TOPK], U32)
        pij, pf = sb("top_side_pos", [P, 2, TT, TOPK], U32), sb("top_side_pos_f", [P, 2, TT, TOPK])
        hot = sb("one_hot", [P, 2, TT * TOPK, TOPK])
        ef, ex = sb("expert_sides", [P, 2, TT, TOPK]), sb("expert_f", [P, TT, TOPK])
        pq = [k.ps(f"query_ps{i}", [P, 512], ctx) for i in range(2)]
        pk = [k.ps(f"score_ps{i}", [P, 512], ctx) for i in range(2)]
        pt = k.ps("keys_turn", [P, 512], ctx)
        names = ("key_in", "key_turn", "key", "q_mm", "q", "s_mm", "s", "scored", "seen")
        s = {n: k.sem(f"route_{n}") for n in names}
        s_w = [k.s_query_w, [k.sem(f"route_w1{i}") for i in range(2)]]
        W = w["w_q_peer"][0].rearrange("(k p) c -> p k c", p=P)
        ident = k.const[:, C_ID:C_ID + P]
        iota = k.const[:, C_IOTA:C_IOTA + TOPK]
        block = ctx.enter_context(nc.Block())

        @block.sync
        def _(sp):
            sp.dma_start(keys[:], w["sub_keys"][0].rearrange("s k c -> k s c")).then_inc(s["key_in"], 16)

            def load(m, first=False):
                col = sp.snap(m * (4 * P)) if not first else 0
                for j in range(2):
                    for i in range(2):
                        if first and j == 0:
                            continue
                        if not first:
                            wait(sp, s["q_mm"], m * 4 - 3 + 2 * j + i)
                        sp.dma_start(wt[j][i][:], W[:, :, bass.ds(col + (2 * j + i) * P, P)]).then_inc(s_w[j][i], 16)

            load(0, True)
            with sp.Fori(1, HEADS // 2) as m:
                load(m)

        @block.tensor
        def _(pe):
            pe.wait_ge(s["key_in"], 16)
            for i in range(2):
                mm = nc.tensor.transpose(pt[:, i * P:(i + 1) * P], keys[:, i, :], ident)
            mm.then_inc(s["key_turn"], 1)
            pe.wait_ge(s["key"], 1)

            def step(m, first=False):
                for j in range(2):
                    for i in range(2):
                        wait(pe, s_w[j][i], m * 16 + 16)
                        if not (first and j == 0):
                            wait(pe, s["q"], m * 4 + 2 * j - 1 + i)
                        for kt in range(KT):
                            mm = nc.tensor.matmul(pq[i][:, 0:SEQ], wt[j][i][:, kt, :], k.h1T[:, kt, :], start=(kt == 0), stop=(kt == KT - 1))
                        mm.then_inc(s["q_mm"], 1)
                    for i in range(2):
                        wait(pe, s["q"], m * 4 + 2 * j + i + 1)
                        if not (first and j == 0):
                            wait(pe, s["s"], m * 4 + 2 * j - 1 + i)
                        for t in range(TT):
                            mm = nc.tensor.matmul(pk[i][:, t * P:(t + 1) * P], qT[i][:, t * P:(t + 1) * P], kT[:, i, :], start=True, stop=True)
                        mm.then_inc(s["s_mm"], 1)

            step(0, True)
            with pe.Fori(1, HEADS // 2) as m:
                step(m)

        @block.scalar
        def _(act):
            act.wait_ge(s["key_turn"], 1)
            nc.scalar.copy(kT[:], pt[:, 0:2 * P].rearrange("p (s c) -> p s c", s=2)).then_inc(s["key"], 1)

            def step(m, first=False):
                for j in range(2):
                    for i in range(2):
                        wait(act, s["q_mm"], m * 4 + 2 * j + i + 1)
                        if not (first and j == 0):
                            wait(act, s["s_mm"], m * 4 + 2 * j + i - 1)
                        nc.scalar.copy(qT[i][:], pq[i][:, 0:SEQ]).then_inc(s["q"], 1)
                    for i in range(2):
                        wait(act, s["s_mm"], m * 4 + 2 * j + i + 1)
                        if not (first and j == 0):
                            wait(act, s["scored"], m * 2 + j)
                        nc.scalar.copy(sc[:, :, i, :], pk[i][:, 0:TT * P].rearrange("p (t k) -> p t k", t=TT)).then_inc(s["s"], 1)

            step(0, True)
            with act.Fori(1, HEADS // 2) as m:
                step(m)

        @block.vector
        def _(dve):
            v, d = nc.vector, nc.vector.drain

            def best16(value, index, values, left, where):
                for o in where:
                    v.max(value(o)[:, 0:8], values(o))
                d()
                for o in where:
                    v.max_index(index(o)[:, 0:8], value(o)[:, 0:8], values(o))
                    ins = v.match_replace(left(o), value(o)[:, 0:8], values(o), NEG)
                d()
                for o in where:
                    v.max(value(o)[:, 8:16], left(o))
                d()
                for o in where:
                    v.max_index(index(o)[:, 8:16], value(o)[:, 8:16], left(o))
                return ins

            def step(m, j):
                wait(dve, s["s"], m * 4 + 2 * j + 2)
                dve.sem_inc(s["seen"], 1)
                sides = [(t, i) for t in range(TT) for i in range(2)]
                best16(lambda o: sv[:, o[0], o[1], :], lambda o: si[:, o[0], o[1], :], lambda o: sc[:, o[0], o[1], :],
                       lambda o: sc2[:, o[0], o[1], :], sides)
                d()
                v.tensor_copy(sif[:], si[:]).then_inc(s["scored"], 1)
                for t in range(TT):
                    v.tensor_tensor(cand[:, t], sv[:, t, 0, :].rearrange("p (a b) -> p a b", b=1).to_broadcast((P, TOPK, TOPK)),
                                    sv[:, t, 1, :].rearrange("p (a b) -> p a b", a=1).to_broadcast((P, TOPK, TOPK)), ALU.add)
                d()
                best16(lambda t: tv[:, t], lambda t: ti[:, t], lambda t: cand[:, t].rearrange("p a b -> p (a b)"), lambda t: cand2[:, t], range(TT))
                d()
                v.tensor_copy(k.gates[:, :, bass.ds(m * 2 + j, 1), :].rearrange("p t a n -> p t (a n)"), tv[:])
                v.tensor_scalar(pij[:, 0], ti[:], 4, None, ALU.logical_shift_right)
                v.tensor_scalar(pij[:, 1], ti[:], 15, None, ALU.bitwise_and)
                d()
                v.tensor_copy(pf[:], pij[:])
                d()
                for i in range(2):
                    v.tensor_tensor(hot[:, i], pf[:, i].rearrange("p t (n a) -> p (t n) a", a=1).to_broadcast((P, TT * TOPK, TOPK)),
                                    iota.rearrange("p (a n) -> p a n", a=1).to_broadcast((P, TT * TOPK, TOPK)), ALU.is_equal)
                d()
                for i in range(2):
                    for t in range(TT):
                        h = hot[:, i, t * TOPK:(t + 1) * TOPK, :]
                        v.tensor_tensor(h, h, sif[:, t, i, :].rearrange("p (a n) -> p a n", a=1).to_broadcast((P, TOPK, TOPK)), ALU.mult)
                d()
                v.tensor_reduce(ef[:].rearrange("p i t n -> p (i t n)"), hot[:].rearrange("p i n c -> p (i n) c"), AX.X, ALU.add)
                d()
                v.scalar_tensor_tensor(out=ex[:], in0=ef[:, 0], scalar=float(N_KEYS), in1=ef[:, 1], op0=ALU.mult, op1=ALU.add)
                d()
                v.tensor_copy(k.idx[:, :, bass.ds(m * 2 + j, 1), :].rearrange("p t a n -> p t (a n)"), ex[:])
                d()

            def steps(m):
                for j in range(2):
                    step(m, j)

            steps(0)
            with dve.Fori(1, HEADS // 2) as m:
                steps(m)


def peer_stage(k, w, out):
    nc = k.nc
    GROUPS = TT * HEADS
    RU, RV, RD = 4, 4, 4
    with ExitStack() as ctx:
        sb = lambda name, shape, dt=F32: k.sb(name, shape, dt, ctx=ctx)
        ur = [sb(f"up_rows{i}", [P, D]) for i in range(RU)]
        vr = [sb(f"down_rows{i}", [P, D]) for i in range(RV)]
        dg = [sb(f"diagonal{i}", [P, P]) for i in range(RD)]
        iu = [sb(f"up_experts{i}", [P, TOPK], I32) for i in range(2)]
        iv = [sb(f"down_experts{i}", [P, TOPK], I32) for i in range(2)]
        gat = [sb(f"group_gates{i}", [P, TOPK]) for i in range(2)]
        dots = [sb(f"dots{i}", [P, TOPK]) for i in range(2)]
        act_ = [sb(f"weights{i}", [P, TOPK]) for i in range(2)]
        aid = sb("alpha_identity", [P, P])
        gam, bet = sb("ln2_gamma", [P, D]), sb("ln2_beta", [P, D])
        y = sb("ln2_y", [P, D])
        mx, ss = sb("gate_sum", [P, TT, HEADS]), sb("gate_rsum", [P, TT, HEADS])
        stats, mv, rs = sb("ln2_stats", [P, 4, 6]), sb("ln2_mv", [P, 2]), sb("ln2_rs", [P, 4])
        ps = [[k.ps(f"peer_ps{t}{n}", [P, 512], ctx) for n in range(4)] for t in range(TT)]
        s_u = [k.sem(f"up_arrived{i}") for i in range(RU)]
        s_v = [k.sem(f"down_arrived{i}") for i in range(RV)]
        names = ("gather", "idx_u", "idx_v", "dot", "gelu", "weight", "diag", "added", "aid", "gb", "y", "var", "root", "norm", "out", "gate", "exp", "shift")
        s = {n: k.sem(f"peer_{n}") for n in names}
        ident = k.const[:, C_ID:C_ID + P]
        block = ctx.enter_context(nc.Block())

        def schedule(eng, step):
            step(0, 0, 0, None)
            step(1, 1, 0, 0)
            with eng.Fori(1, HEADS // 2) as m:
                step(m * 2, 0, 0, 0)
                step(m * 2 + 1, 1, 0, 0)
            step(8, 0, 1, 0)
            with eng.Fori(0, 3) as m:
                step(m * 2 + 9, 1, 1, 1)
                step(m * 2 + 10, 0, 1, 1)
            step(15, 1, 1, 1)
            step(16, 0, None, 1)

        @block.sync
        def _(sp):
            sp.dma_start(gam[:], row_broadcast(w["ln2_g"][0])).then_inc(s["gb"], 16)
            sp.dma_start(bet[:], row_broadcast(w["ln2_b"][0])).then_inc(s["gb"], 16)
            for t in range(TT):
                sp.wait_ge(s["norm"], t + 1)
                sp.dma_start(out[0, t * P:(t + 1) * P, :], y[:]).then_inc(s["out"], 16)
            sp.wait_ge(s["out"], 16 * TT)

        @block.gpsimd
        def _(pool):
            def gather(rows, table, ix, j, arrived):
                pool.sem_inc(s["gather"], 1)
                pool.indirect_dma_start(rows[:], None, table, bass.IndirectOffsetOnAxis(ap=ix[:, j:j + 1], axis=0)).then_inc(arrived, 16)

            def step(g, par, tu, tv):
                flat = k.idx[:].rearrange("p t h n -> p (t h) n")
                if tu is not None:
                    nc.gpsimd.tensor_copy(iu[par][:], flat[:, bass.ds(g, 1), :].rearrange("p a n -> p (a n)")).then_inc(s["idx_u"], 1)
                if tv is not None:
                    nc.gpsimd.tensor_copy(iv[par][:], flat[:, bass.ds(g - 1, 1), :].rearrange("p a n -> p (a n)")).then_inc(s["idx_v"], 1)
                if tu is not None:
                    wait(pool, s["idx_u"], g + 1)
                if tv is not None:
                    wait(pool, s["idx_v"], g)
                for j in range(TOPK):
                    if tu is not None:
                        if not isinstance(g, int) or g * TOPK + j >= RU:
                            wait(pool, s["dot"], g * TOPK + (j - RU + 1))
                        gather(ur[j % RU], w["u_table"][0], iu[par], j, s_u[j % RU])
                    if tv is not None:
                        if not isinstance(g, int) or (g - 1) * TOPK + j >= RV:
                            wait(pool, s["added"], (g - 1) * TOPK + (j - RV + 1))
                        gather(vr[j % RV], w["v_table"][0], iv[par], j, s_v[j % RV])

            schedule(pool, step)

        @block.vector
        def _(dve):
            v, d = nc.vector, nc.vector.drain
            v.tensor_scalar(aid[:], ident, ALPHA, None, ALU.mult).then_inc(s["aid"], 1)

            def finish(t):
                if t:
                    dve.wait_ge(s["out"], 16 * t)
                for n in range(4):
                    v.tensor_copy(y[:, n * 512:(n + 1) * 512], ps[t][n][:])
                d()
                norm_stats(nc, y[:, :], P, stats, mv, rs).then_inc(s["var"], 1)
                dve.wait_ge(s["root"], t + 1)
                norm_apply(nc, y[:, :], P, mv, rs, gam, bet).then_inc(s["norm"], 1)

            def step(g, par, tu, tv):
                if tu is not None:
                    if not isinstance(g, int) or g >= 2:
                        wait(dve, s["diag"], (g - 1) * TOPK)
                    x = k.gates[:].rearrange("p t h n -> p (t h) n")[:, bass.ds(g, 1), :].rearrange("p a n -> p (a n)")
                    v.tensor_copy(gat[par][:], x).then_inc(s["gate"], 1)
                    for j in range(TOPK):
                        wait(dve, s_u[j % RU], g * (16 * TOPK // RU) + 16 * (j // RU + 1))
                        v.tensor_tensor_reduce(ur[j % RU][:], ur[j % RU][:], k.h[:, tu, :], 1.0, 0.0, ALU.mult, ALU.add,
                                               dots[par][:, j:j + 1]).then_inc(s["dot"], 1)
                    wait(dve, s["gelu"], g + 1)
                    v.tensor_tensor(act_[par][:], dots[par][:], gat[par][:], ALU.mult).then_inc(s["weight"], 1)
                if isinstance(g, int) and g in (HEADS, GROUPS):
                    wait(dve, s["added"], g * TOPK)
                    if g == HEADS:
                        dve.wait_ge(s["gb"], 32)
                    finish(g // HEADS - 1)

            g = k.gates[:].rearrange("p t h n -> p (t h) n")
            flat = lambda x: x[:].rearrange("p t h -> p (t h)")
            v.tensor_copy(flat(mx), g[:, :, 0])
            d()
            wide = lambda x: x[:].rearrange("p t (h n) -> p (t h) n", n=1).to_broadcast((P, TT * HEADS, TOPK))
            v.tensor_tensor(g, g, wide(mx), ALU.subtract).then_inc(s["shift"], 1)
            dve.wait_ge(s["exp"], 1)
            v.tensor_reduce(flat(mx), g, AX.X, ALU.add)
            d()
            v.reciprocal(flat(ss), flat(mx))
            d()
            v.tensor_tensor(g, g, wide(ss), ALU.mult)
            d()
            schedule(dve, step)

        @block.scalar
        def _(act):
            def step(g, par, tu, tv):
                if tv is not None:
                    wait(act, s["weight"], g)
                    for j in range(TOPK):
                        if not isinstance(g, int) or (g - 1) * TOPK + j >= RD:
                            wait(act, s["added"], (g - 1) * TOPK + (j - RD + 1))
                        nc.scalar.activation(dg[j % RD][:], ident, ACT.Copy, scale=act_[1 - par][:, j:j + 1]).then_inc(s["diag"], 1)
                if tu is not None:
                    wait(act, s["dot"], g * TOPK + TOPK)
                    nc.scalar.activation(dots[par][:], dots[par][:], ACT.Gelu).then_inc(s["gelu"], 1)
                if isinstance(g, int) and g in (HEADS, GROUPS):
                    act.wait_ge(s["var"], g // HEADS)
                    nc.scalar.activation(rs[:, 2:3], rs[:, 1:2], ACT.Sqrt).then_inc(s["root"], 1)

            act.wait_ge(s["shift"], 1)
            nc.scalar.activation(k.gates[:], k.gates[:], ACT.Exp).then_inc(s["exp"], 1)
            schedule(act, step)

        @block.tensor
        def _(pe):
            pe.wait_ge(s["aid"], 1)
            for t in range(TT):
                for n in range(4):
                    nc.tensor.matmul(ps[t][n][:], aid[:], k.h[:, t, n * 512:(n + 1) * 512], start=True, stop=False, skip_group_check=True)

            def step(g, par, tu, tv):
                if tv is None:
                    return
                last = isinstance(g, int) and g in (HEADS, GROUPS)
                for j in range(TOPK):
                    wait(pe, s_v[j % RV], (g - 1) * (16 * TOPK // RV) + 16 * (j // RV + 1))
                    wait(pe, s["diag"], (g - 1) * TOPK + j + 1)
                    for n in range(4):
                        mm = nc.tensor.matmul(ps[tv][n][:], dg[j % RD][:], vr[j % RV][:, n * 512:(n + 1) * 512], start=False,
                                              stop=(last and j == TOPK - 1), skip_group_check=True)
                    mm.then_inc(s["added"], 1)

            schedule(pe, step)


def program(nc, w, out):
    ctx = ExitStack()
    with ctx:
        k = Core(nc, ctx)
        k.lora_tiles = ((LORA0, DECAY_LORA), (LORA0 + DECAY_LORA, ICL_LORA),
                        (POOL0 - GATE_LORA, P), (POOL0 - P, P))
        k.const = k.sb("constants", [P, NCONST])
        k.h = k.sb("h", [P, TT, D])
        k.vec = k.sb("vectors", [P, NVEC, PAIRS])
        k.pool_scale = k.sb("pool_scale_t", [P, POOL_DIM // P])
        k.mu_lora = k.sb("mu_lora", [P, 4])
        k.om_lora = k.sb("one_minus_mu_lora", [P, 4])
        k.idx = k.sb("experts", [P, TT, HEADS, TOPK], I32)
        k.gates = k.sb("gates", [P, TT, HEADS, TOPK])
        with ExitStack() as front:
            k.yaT = k.sb("yaT", [P, KT, SEQ], ctx=front)
            k.hT = k.sb("hT", [P, KT, T], ctx=front)
            k.hT_high = k.sb("hT_high", [P, KT, T], ctx=front)
            k.lora = k.sb("lora", [P, 4, T], ctx=front)
            with ExitStack() as early:
                k.lora_raw = k.sb("lora_weights", [P, KT, POOL0 - LORA0], ctx=early)
                k.s_lora_w = [k.sem(f"lora_w{g}") for g in range(4)]
                input_stage(k, w)
                lora_stage(k, w)
            rwkv_stage(k, w)
            k.release_sems()
            k.ybT = k.sb("ybT", [P, KT // 2, SEQ], ctx=front)
            k.ybT_high = k.sb("ybT_high", [P, KT // 2, SEQ], ctx=front)
            k.pool_tmp = k.sb("pool_tmp", [P, 2, T], ctx=front)
            pool_stage(k, w)
            k.mT = k.sb("mergedT", [P, KT, SEQ], ctx=front)
            k.mT_high = k.sb("mergedT_high", [P, KT, SEQ], ctx=front)
            k.out_raw = [k.sb(f"out_w{i}", [P, 4, 512], ctx=front) for i in range(2)]
            k.s_out_w = [k.sem(f"out_w{i}") for i in range(2)]
            k.query_raw = [x[:].rearrange("p a (b c) -> p (a b) c", c=P) for x in k.out_raw]
            k.s_query_w = [k.sem(f"query_w{i}") for i in range(2)]
            merge_stage(k, w)
            k.h1T = k.yaT
            out_stage(k, w)
            router_stage(k, w)
        peer_stage(k, w, out)



_INS = ["x", "meta_tokens", "ln_in_g", "ln_in_b", "w_in", "mu_shift", "w0", "w_w2", "a0", "w_a2", "w_g2", "k_k", "k_a", "r_k",
        "gn_g", "gn_b", "w_pool", "pool_scale", "b_gate", "w_branch_a", "w_branch_b", "w_out", "ln1_g", "ln1_b", "w_q_peer",
        "sub_keys", "u_table", "v_table", "ln2_g", "ln2_b"]


def kernel(**inputs):
    import numpy as _np
    import concourse.bacc as _bacc
    from concourse import mybir as _mybir
    from concourse.bass_utils import run_bass_kernel_spmd as _run

    nc = _bacc.Bacc("TRN2", target_bir_lowering=False, num_devices=1)
    arrays = {f"in_{n}": _np.ascontiguousarray(inputs[n]) for n in _INS}
    arrays["in_consts"] = constants()
    w = {n[3:]: nc.dram_tensor(n, a.shape, _mybir.dt.from_np(a.dtype), kind="ExternalInput").ap() for n, a in arrays.items()}
    out = nc.dram_tensor("out", (1, SEQ, D), F32, kind="ExternalOutput").ap()
    program(nc, w, out)
    r = _run(nc, [arrays], core_ids=[0])
    return r.results[0]["out"]
```
